# Optimizing a Trainium2 kernel written in Bass

```python
import math
import jax, jax.numpy as jnp
from jax import lax
import numpy as np

D_MODEL = 2048
BATCH = 1
SEQ = 256
DEPTH = 1

CHUNK = 64
D_MIX = D_MODEL
D_LRU = D_MIX // 2
N_LRU_HEADS = 8
LRU_HEAD_DIM = D_LRU // N_LRU_HEADS
D_SC = D_MIX - D_LRU
N_SC_GROUPS = 16
SC_GROUP_DIM = D_SC // N_SC_GROUPS
LRU_CONV_W = 4
SC_CONV_W = 3
RG_C = 8.0
D_FF = 5632
EPS = 1e-6
D_IN = 2 * D_LRU + 3 * D_SC

kernel_name = "hybrid_rglru_shortconv_macaron_block"

def rmsnorm(x, g):
    xf = x.astype(jnp.float32)
    y = xf * lax.rsqrt(jnp.mean(xf * xf, axis=-1, keepdims=True) + EPS)
    return (y * g.astype(jnp.float32)).astype(x.dtype)

def swiglu(x, w_gate, w_up, w_down):
    return (jax.nn.silu(x @ w_gate) * (x @ w_up)) @ w_down

def causal_dwconv(x, w, b=None):
    k_w = w.shape[0]
    s = x.shape[1]
    xp = jnp.pad(x, ((0, 0), (k_w - 1, 0), (0, 0)))
    y = xp[:, 0:s] * w[0]
    for k in range(1, k_w):
        y = y + xp[:, k:k + s] * w[k]
    if b is not None:
        y = y + b
    return y

def rg_lru(x, w_r, b_r, w_i, b_i, lam):
    bsz, s, _ = x.shape
    xh = x.reshape(bsz, s, N_LRU_HEADS, LRU_HEAD_DIM)
    r = jax.nn.sigmoid(jnp.einsum('bshd,hde->bshe', xh, w_r) + b_r).reshape(bsz, s, D_LRU)
    i = jax.nn.sigmoid(jnp.einsum('bshd,hde->bshe', xh, w_i) + b_i).reshape(bsz, s, D_LRU)
    log_a = -RG_C * r.astype(jnp.float32) * jax.nn.softplus(-lam.astype(jnp.float32))
    a = jnp.exp(log_a)
    mult = jnp.sqrt(-jnp.expm1(2.0 * log_a))
    b = mult * (i.astype(jnp.float32) * x.astype(jnp.float32))

    def combine(left, right):
        a_l, b_l = left
        a_r, b_r_ = right
        return a_l * a_r, a_r * b_l + b_r_

    _, h = lax.associative_scan(combine, (a, b), axis=1)
    return h.astype(x.dtype)

def setup_inputs(seed: int = 0) -> dict:
    key = jax.random.key(seed)
    ks = jax.random.split(key, 32)
    f32 = jnp.float32

    def nrm(k, shape, fan_in):
        return jax.random.normal(k, shape, f32) * (fan_in ** -0.5)

    def gain(k, shape):
        return 1.0 + 0.05 * jax.random.normal(k, shape, f32)

    L = DEPTH
    u = jax.random.uniform(ks[20], (L, D_LRU), f32, 0.9, 0.999)
    a0 = u ** (1.0 / RG_C)
    lam = jnp.log(a0) - jnp.log1p(-a0)
    return {
        "x": jax.random.normal(ks[0], (BATCH, SEQ, D_MODEL), f32),
        "ffn1_pre_g": gain(ks[1], (L, D_MODEL)),
        "ffn1_w_gate": nrm(ks[2], (L, D_MODEL, D_FF), D_MODEL),
        "ffn1_w_up": nrm(ks[3], (L, D_MODEL, D_FF), D_MODEL),
        "ffn1_w_down": nrm(ks[4], (L, D_FF, D_MODEL), D_FF),
        "ffn1_post_g": gain(ks[5], (L, D_MODEL)),
        "mix_pre_g": gain(ks[6], (L, D_MODEL)),
        "w_in": nrm(ks[7], (L, D_MODEL, D_IN), D_MODEL),
        "lru_conv_w": nrm(ks[8], (L, LRU_CONV_W, D_LRU), LRU_CONV_W),
        "lru_conv_b": 0.01 * jax.random.normal(ks[9], (L, D_LRU), f32),
        "lru_w_r": nrm(ks[10], (L, N_LRU_HEADS, LRU_HEAD_DIM, LRU_HEAD_DIM), LRU_HEAD_DIM),
        "lru_b_r": 0.01 * jax.random.normal(ks[11], (L, N_LRU_HEADS, LRU_HEAD_DIM), f32),
        "lru_w_i": nrm(ks[12], (L, N_LRU_HEADS, LRU_HEAD_DIM, LRU_HEAD_DIM), LRU_HEAD_DIM),
        "lru_b_i": 0.01 * jax.random.normal(ks[13], (L, N_LRU_HEADS, LRU_HEAD_DIM), f32),
        "lru_lambda": lam,
        "sc_conv_w": nrm(ks[14], (L, SC_CONV_W, D_SC), SC_CONV_W),
        "w_out": nrm(ks[15], (L, D_MIX, D_MODEL), D_MIX),
        "mix_post_g": gain(ks[16], (L, D_MODEL)),
        "ffn2_pre_g": gain(ks[17], (L, D_MODEL)),
        "ffn2_w_gate": nrm(ks[18], (L, D_MODEL, D_FF), D_MODEL),
        "ffn2_w_up": nrm(ks[19], (L, D_MODEL, D_FF), D_MODEL),
        "ffn2_w_down": nrm(ks[21], (L, D_FF, D_MODEL), D_FF),
        "ffn2_post_g": gain(ks[22], (L, D_MODEL)),
    }

def reference(x, ffn1_pre_g, ffn1_w_gate, ffn1_w_up, ffn1_w_down, ffn1_post_g,
              mix_pre_g, w_in, lru_conv_w, lru_conv_b, lru_w_r, lru_b_r, lru_w_i, lru_b_i,
              lru_lambda, sc_conv_w, w_out, mix_post_g,
              ffn2_pre_g, ffn2_w_gate, ffn2_w_up, ffn2_w_down, ffn2_post_g):
    h = x
    for l in range(DEPTH):
        f = swiglu(rmsnorm(h, ffn1_pre_g[l]), ffn1_w_gate[l], ffn1_w_up[l], ffn1_w_down[l])
        h = h + 0.5 * rmsnorm(f, ffn1_post_g[l])

        u = rmsnorm(h, mix_pre_g[l])
        z = u @ w_in[l]
        o = np.cumsum([0, D_LRU, D_LRU, D_SC, D_SC, D_SC]).tolist()
        lru_x = z[..., o[0]:o[1]]
        lru_gate = z[..., o[1]:o[2]]
        sc_b = z[..., o[2]:o[3]]
        sc_c = z[..., o[3]:o[4]]
        sc_x = z[..., o[4]:o[5]]

        xc = causal_dwconv(lru_x, lru_conv_w[l], lru_conv_b[l])
        y_lru = rg_lru(xc, lru_w_r[l], lru_b_r[l], lru_w_i[l], lru_b_i[l], lru_lambda[l])
        y_lru = y_lru * jax.nn.gelu(lru_gate)

        y_sc = sc_b * causal_dwconv(sc_c * sc_x, sc_conv_w[l])

        y = jnp.concatenate([y_lru, y_sc], axis=-1) @ w_out[l]
        h = h + rmsnorm(y, mix_post_g[l])

        f = swiglu(rmsnorm(h, ffn2_pre_g[l]), ffn2_w_gate[l], ffn2_w_up[l], ffn2_w_down[l])
        h = h + 0.5 * rmsnorm(f, ffn2_post_g[l])
    return h


_drawn_inputs = setup_inputs


def setup_inputs(seed=0):
    import zlib

    import numpy as np

    out = dict(_drawn_inputs(seed))
    spreads = {}
    factors = {'lru_conv_b': 3.309, 'lru_b_r': 64.0, 'lru_b_i': 52.549, 'ffn2_post_g': 3.577}
    for name, (base, spread) in spreads.items():
        noise = np.random.default_rng([zlib.crc32(name.encode()), seed]).standard_normal(out[name].shape)
        drawn = base * np.exp(spread * noise) if base else spread * noise
        out[name] = __import__('jax').numpy.asarray(drawn.astype(out[name].dtype))
    for name, factor in factors.items():
        out[name] = (out[name] * factor).astype(out[name].dtype)
    return out
```

```python
import concourse.bass as bass
from concourse import mybir
from contextlib import ExitStack


P = 128
TOK = 2
W = 512
GK = 2
SLOTS = 4
EPS = 1e-6


def hybrid_block_kernel(nc, x, f1_pre, f1_wg, f1_wu, f1_wd, f1_post, mix_pre, w_in, conv_w, conv_b,
                        w_r, b_r, w_i, b_i, lam, sc_w, w_out, mix_post, f2_pre, f2_wg, f2_wu, f2_wd,
                        f2_post, out):
    f32, f32r = mybir.dt.float32, mybir.dt.float32r
    ALU, ACT, AX = mybir.AluOpType, mybir.ActivationFunctionType, mybir.AxisListType
    ds = bass.ds

    D, F = f1_wg.shape[1], f1_wg.shape[2]
    DIN = w_in.shape[2]
    DL = lam.shape[1]
    HEADS = w_r.shape[1]
    TAPS_A, TAPS_B = conv_w.shape[1], sc_w.shape[1]
    T = TOK * P
    KD, KF = D // P, F // P
    MC = W // P
    NC = D // W
    FC = F // W
    JC = DL // W
    GP, GF = KD // GK, KF // GK
    assert x.shape == (1, T, D) and DIN == 5 * DL and 2 * DL == D and JC == 2 and HEADS == DL // P
    assert GP == 2 * SLOTS and GF == 22 and NC == 4

    four = [j % SLOTS for j in range(GP)]
    short = 2 * (SLOTS - 1)
    odd = [j % (SLOTS - 1) for j in range(short)] + [j % SLOTS for j in range(GF - short)]
    slots, starts = [], {}
    for name, n, pattern in (("up1", 2 * FC, four), ("down1", NC, odd), ("in", 5 * JC, four),
                             ("out", NC, four), ("up2", 2 * FC, four), ("down2", NC, odd)):
        starts[name] = len(slots)
        slots += pattern * n
    starts["end"] = len(slots)
    before, uses, last_use, count = [], [], [None] * SLOTS, [0] * SLOTS
    for g, s in enumerate(slots):
        before.append(last_use[s])
        count[s] += 1
        uses.append(count[s])
        last_use[s] = g

    class Place:

        def __init__(self, g0, it=0, stride=0):
            self.g0, self.it, self.stride = g0, it, stride

        def slot(self, j):
            return slots[self.g0 + j]

        def count(self, j):
            return self.it * self.stride + (self.g0 + j + 1)

        def first(self, j):
            return before[self.g0 + j] is None

        def freed(self, j):
            return self.it * self.stride + (before[self.g0 + j] + 1)

        def loaded(self, j):
            g = self.g0 + j
            per = 16 * (uses[g + self.stride] - uses[g]) if self.stride else 0
            return self.it * per + 16 * uses[g]

    def rows(w):
        return w[0].rearrange("(k p) n -> p k n", p=P)

    ffn_w = {0: (rows(f1_wg), rows(f1_wu), rows(f1_wd)), 1: (rows(f2_wg), rows(f2_wu), rows(f2_wd))}
    w_in_v, w_out_v = rows(w_in), rows(w_out)
    x_v, out_v = rows(x), rows(out)

    ctx = ExitStack()
    with ctx:
        def sb(name, shape, dt=f32):
            return ctx.enter_context(nc.sbuf_tensor(name, shape, dt))

        def sem(name):
            return ctx.enter_context(nc.semaphore(name))

        raw = sb("raw", [P, SLOTS, GK, W])
        w_hi = sb("w_hi", [P, SLOTS, GK, W], f32r)
        w_lo = sb("w_lo", [P, SLOTS, GK, W], f32r)
        xT_hi = sb("xT_hi", [P, KD, T], f32r)
        xT_lo = sb("xT_lo", [P, KD, T], f32r)
        resid = sb("resid", [P, TOK, D])
        gpost = sb("gpost", [P, D])
        act_g = sb("act_g", [P, TOK, W])
        hid = sb("hid", [P, TOK, W])
        gained = sb("gained", [P, MC, P])
        ident = sb("ident", [P, P])
        NB = 2 * KD + (TAPS_A + 4 + TAPS_B) * HEADS
        small_a = sb("small_a", [KD, P])
        small_b = sb("small_b", [NB, P])
        cst = sb("cst", [P, KD + NB])
        sums = sb("sums", [P, 2, TOK, NC])
        tot = sb("tot", [P, 2, TOK])
        mean = sb("mean", [P, 2, TOK])
        rstd = sb("rstd", [P, 2, TOK])
        power = sb("power", [P, TOK])
        soft = sb("soft", [P, 5, HEADS])
        sp4 = sb("sp4", [P, HEADS])

        region_at = (nc.sbuf_base + 31) // 32 * 32
        region_size = 4 * 2 * KF * T
        sb("region", [P, 2 * KF * T])

        def at(name, shape, offset, dt=f32):
            size = 4
            for n in shape[1:]:
                size *= n
            assert offset + size <= region_size
            return nc.alloc_sbuf_tensor_at(name, shape, dt, offset=region_at + offset), offset + size

        hT_hi, o = at("hT_hi", [P, KF, T], 0, f32r)
        hT_lo, o = at("hT_lo", [P, KF, T], o, f32r)
        o = 4 * KD * T
        pad = TAPS_A - 1
        xc, o = at("xc", [P, MC, T], o)
        rr, o = at("rr", [P, MC, T], o)
        ii, o = at("ii", [P, MC, T], o)
        gl0, o = at("gl0", [P, MC, T], o)
        gl1, o = at("gl1", [P, MC, T], o)
        xpad, o = at("xpad", [P, MC, pad + T], o)
        assert o <= 4 * KF * T
        o = 4 * KF * T + 4 * KD * T
        aa, o = at("aa", [P, MC, T], o)
        bb, o = at("bb", [P, MC, T], o)
        cc, o = at("cc", [P, MC, T], o)
        yc, o = at("yc", [P, MC, T], o)
        yy, o = at("yy", [P, MC, T], o)
        w_ri, o = at("w_ri", [P, 2, HEADS, P], o)
        gl = (gl0, gl1)

        ps = ctx.enter_context(nc.psum_tensor("ps", [P, 8 * W], f32))
        XP, HD = 4, 6

        def bank(n, width=W, start=0):
            if isinstance(n, int):
                return ps[:, n * W + start:n * W + start + width]
            return ps[:, ds(n * W + start, width)]

        def columns(n, width=W):
            return slice(n * width, n * width + width) if isinstance(n, int) else ds(n * width, width)

        def part(t):
            return slice(t * P, t * P + P)

        raw_full = [sem(f"raw_full{s}") for s in range(SLOTS)]
        hi_ready = sem("hi_ready")
        lo_ready = sem("lo_ready")
        w_used = sem("w_used")
        tok0_done = sem("tok0_done")
        x_in = [sem(f"x_in{n}") for n in range(4)]
        small_a_in, small_b_in = sem("small_a_in"), sem("small_b_in")
        heads_in, gpost_in = sem("heads_in"), sem("gpost_in")
        pool_set = sem("pool_set")
        pads_set = sem("pads_set")
        small_xp = sem("small_xp")
        cst_ready = sem("cst_ready")
        sq_done = sem("sq_done")
        fg_done = sem("fg_done")
        tot_post, mean_post = sem("tot_post"), sem("mean_post")
        rstd_post = sem("rstd_post")
        resid_new = sem("resid_new")
        blk_xp = sem("blk_xp")
        blk_gain = sem("blk_gain")
        blk_hi = sem("blk_hi")
        blk_lo = sem("blk_lo")
        blk_sq = sem("blk_sq")
        tot_pre, mean_pre = sem("tot_pre"), sem("mean_pre")
        rstd_pre = sem("rstd_pre")
        silu_done = sem("silu_done")
        hid_done = sem("hid_done")
        hid_xp = sem("hid_xp")
        hT_hi_done = sem("hT_hi_done")
        hT_lo_done = sem("hT_lo_done")
        z_out = sem("z_out")
        z_xp = sem("z_xp")
        z_taken = sem("z_taken")
        step = sem("step")
        lam_neg = sem("lam_neg")
        lam_sig = sem("lam_sig")
        xc_ready = sem("xc_ready")
        head_mm = sem("head_mm")
        head_sig = sem("head_sig")
        tanh_done = sem("tanh_done")
        sqrt_done = sem("sqrt_done")
        y_ready = sem("y_ready")
        y_hi = sem("y_hi")
        y_lo = sem("y_lo")
        stored = sem("stored")

        BLOCKS = [(0, 0), (0, 1), (1, 0), (1, 1), (0, 2), (0, 3), (1, 2), (1, 3)]
        NBLK = len(BLOCKS)
        CONV_W, CONV_B, B_R, B_I, LAM, SC_W = (
            3 * KD + HEADS * n for n in (0, TAPS_A, TAPS_A + 1, TAPS_A + 2, TAPS_A + 3, TAPS_A + 4))
        PHASE = ("up1", "in", "up2")
        Z = [(kind, jc) for kinds in (("gate", "lru"), ("c", "x", "b")) for jc in range(JC) for kind in kinds]
        Z_COL = {kind: n * DL for n, kind in enumerate(("lru", "gate", "b", "c", "x"))}
        NZ = len(Z)
        Z_SCALE = {(q + 1, 3): q for q in range(NZ)}
        Z_TAKE = {(q + 2, 0): q for q in range(NZ - 1)}
        del Z_TAKE[8, 0]
        Z_TAKE[8, 3] = 6
        Z_TAKE[NZ, 5] = NZ - 1
        Y_PART = {(6, 6): 0, (8, 0): 1, (8, 5): 2, (NZ, 5): 3}

        block = ctx.enter_context(nc.Block())

        @block.sync
        def _(sync):
            def load(pl, j, src):
                s = pl.slot(j)
                if not pl.first(j):
                    sync.wait_ge(lo_ready, pl.freed(j))
                sync.dma_start(raw[:, s], src).then_inc(raw_full[s], 16)

            def load_gain(g):
                sync.dma_start(gpost[:], g.broadcast_to([P, D])).then_inc(gpost_in, 16)

            def load_small_b():
                row = 0
                for a, n in ((mix_pre[0].rearrange("(k p) -> k p", p=P), KD), (f2_pre[0].rearrange("(k p) -> k p", p=P), KD)):
                    sync.dma_start(small_b[row:row + n, :], a).then_inc(small_b_in, 16)
                    row += n
                for a, n in ((conv_w[0].rearrange("t (k p) -> (t k) p", p=P), TAPS_A),
                             (conv_b[0].rearrange("(k p) -> k p", p=P), 1), (b_r[0], 1), (b_i[0], 1),
                             (lam[0].rearrange("(k p) -> k p", p=P), 1),
                             (sc_w[0].rearrange("t (k p) -> (t k) p", p=P), TAPS_B)):
                    sync.dma_start(small_b[row:row + n * HEADS, :], a).then_inc(small_b_in, 16)
                    row += n * HEADS

            def load_chunk(pl, w, c, js):
                for j in js:
                    load(pl, j, w[:, GK * j:GK * j + GK, columns(c)])

            def ffn(f):
                up, down = starts[f"up{f + 1}"], starts[f"down{f + 1}"]
                w_gate, w_up, w_down = ffn_w[f]
                for j in range(GP):
                    for n in ({0: (0,), 2: (2,), 4: (1, 3)}.get(j, ()) if f == 0 else ()):
                        t, h = n // 2, n % 2
                        cols = slice(h * D // 2, (h + 1) * D // 2)
                        sync.dma_start(resid[:, t, cols], x_v[:, t, cols]).then_inc(x_in[n], 16)
                    load_chunk(Place(up), w_gate, 0, [j])
                if f == 0:
                    load_small_b()
                if f == 1:
                    sync.wait_ge(fg_done, 2 * TOK * NC)
                load_gain((f1_post, f2_post)[f])
                load_chunk(Place(up + GP), w_up, 0, range(GP))
                with sync.Fori(0, FC - 1) as it:
                    load_chunk(Place(up + 2 * GP, it, 2 * GP), w_gate, it + 1, range(GP))
                    load_chunk(Place(up + 3 * GP, it, 2 * GP), w_up, it + 1, range(GP))
                load_chunk(Place(down), w_down, 0, range(GF))
                with sync.Fori(0, NC - 1) as it:
                    load_chunk(Place(down + GF, it, GF), w_down, it + 1, range(GF))

            ffn(0)
            for q, (kind, jc) in enumerate(Z):
                if q == 1:
                    sync.wait_ge(fg_done, TOK * NC)
                    load_gain(mix_post)
                    sync.wait_ge(w_used, starts["in"])
                    for m, w in enumerate((w_r, w_i)):
                        sync.dma_start(w_ri[:, m], w[0].rearrange("h d e -> d h e")).then_inc(heads_in, 16)
                load_chunk(Place(starts["in"] + GP * q), w_in_v, Z_COL[kind] // W + jc, range(GP))
            load_chunk(Place(starts["out"]), w_out_v, 0, range(GP))
            with sync.Fori(0, NC - 1) as it:
                load_chunk(Place(starts["out"] + GP, it, GP), w_out_v, it + 1, range(GP))
            ffn(1)
            for n in range(TOK * NC):
                t, c = n // NC, n % NC
                sync.wait_ge(resid_new, 2 * NBLK + n + 1)
                sync.dma_start(out_v[:, t, columns(c)], resid[:, t, columns(c)]).then_inc(stored, 16)
            sync.wait_ge(stored, 16 * TOK * NC)

        @block.gpsimd
        def _(pool):
            pool.memset(power[:], -0.5).then_inc(pool_set, 1)
            pool.memset(ident[:], 0.0).then_inc(pool_set, 1)
            pool.wait_ge(pool_set, 2)
            pool.affine_select(out=ident[:], in_=ident[:], compare_op=ALU.not_equal, fill=1.0, base=0,
                               pattern=[[-1, P]], channel_multiplier=1).then_inc(pool_set, 1)

            def post(d):
                for t in range(TOK):
                    pool.wait_ge(mean_post, TOK * d + t + 1)
                    pool.tensor_tensor(rstd[:, 0, t:t + 1], mean[:, 0, t:t + 1], power[:, 0:1],
                                       ALU.pow).then_inc(rstd_post, 1)

            def pre(r):
                pool.wait_ge(mean_pre, r + 1)
                pool.tensor_tensor(rstd[:, 1, :], mean[:, 1, :], power[:], ALU.pow).then_inc(rstd_pre, 1)

            pre(0)
            post(0)
            pool.wait_ge(w_used, starts["in"])
            pool.memset(xpad[:, :, 0:pad], 0.0).then_inc(pads_set, 1)
            pre(1)
            post(1)
            pre(2)
            post(2)

        @block.scalar
        def _(act):
            sc = nc.scalar
            act.dma_start(small_a[:], f1_pre[0].rearrange("(k p) -> k p", p=P)).then_inc(small_a_in, 16)
            def split(pl, j):
                s = pl.slot(j)
                act.wait_ge(raw_full[s], pl.loaded(j))
                if not pl.first(j):
                    act.wait_ge(w_used, pl.freed(j))
                sc.copy(w_hi[:, s], raw[:, s]).then_inc(hi_ready, 1)

            def bank_square(n, t):
                sc.activation(act_g[:, t], bank(n * 2 + t), ACT.Square,
                              accum_out=sums[:, 0, t, (slice(n, n + 1) if isinstance(n, int) else ds(n, 1))]
                              ).then_inc(sq_done, 1)

            def last_square(d, t):
                if t == 0:
                    act.wait_ge(tok0_done, NC * (d + 1))
                else:
                    act.wait_ge(w_used, starts[("in", "up2", "end")[d]])
                bank_square(NC - 1, t)

            def block_parts(r, k):
                t, c = BLOCKS[k]
                act.wait_ge(blk_gain, NBLK * r + k + 1)
                sc.copy(xT_hi[:, MC * c:MC * c + MC, part(t)], gained[:]).then_inc(blk_hi, 1)
                if r:
                    act.wait_ge(resid_new, NBLK * (r - 1) + k + 1)
                if k or r:
                    act.wait_ge(blk_sq, NBLK * r + k)
                sc.activation(act_g[:, t], resid[:, t, columns(c)], ACT.Square,
                              accum_out=sums[:, 1, t, c:c + 1]).then_inc(blk_sq, 1)

            def hand_over(r):
                pl = Place(starts[PHASE[r]])
                if r:
                    last_square(r - 1, 0)
                for what, n in (("split", 0), ("split", 1), ("block", 0), ("split", 2), ("square", 1),
                                ("block", 1), ("split", 3), ("block", 2), ("block", 3), ("block", 4),
                                ("split", 4), ("split", 5), ("block", 5), ("split", 6), ("split", 7),
                                ("block", 6), ("block", 7)):
                    if what == "split":
                        split(pl, n)
                    elif what == "block":
                        block_parts(r, n)
                    elif r:
                        last_square(r - 1, 1)

            def hidden_hi(f, c):
                for t in range(TOK):
                    act.wait_ge(hid_xp, c * TOK + (f * FC * TOK + t + 1))
                    sc.copy(hT_hi[:, (slice(c * MC, c * MC + MC) if isinstance(c, int) else ds(c * MC, MC)), part(t)],
                            bank(XP + t).rearrange("p (m q) -> p m q", q=P)).then_inc(hT_hi_done, 1)

            def up_groups(f, pl, c, js, tail):
                for j in js:
                    if tail and j == GP:
                        hidden_hi(f, c - 1)
                    if j == GP + 3:
                        act.wait_ge(w_used, pl.count(GP - 1))
                        act.wait_ge(rstd_pre, 1 + 2 * f)
                        if tail or f:
                            act.wait_ge(hid_done, c * TOK + f * FC * TOK)
                        for t in range(TOK):
                            sc.activation(act_g[:, t], bank(t), ACT.Silu, scale=rstd[:, 1, t:t + 1]
                                          ).then_inc(silu_done, 1)
                    split(pl, j)

            def summed_chunks(g0, n_groups, hook):
                with act.Fori(0, NC - 1) as it:
                    pl = Place(g0 + n_groups, it, n_groups)
                    for j in range(n_groups):
                        if j == hook:
                            act.wait_ge(w_used, pl.count(-1))
                            for t in range(TOK):
                                bank_square(it, t)
                        split(pl, j)

            def ffn(f):
                up, down = starts[f"up{f + 1}"], starts[f"down{f + 1}"]
                hand_over(2 * f)
                if f == 0:
                    act.wait_ge(lam_neg, 1)
                    sc.activation(soft[:, 1], soft[:, 0], ACT.Sigmoid).then_inc(lam_sig, 1)
                up_groups(f, Place(up), 0, range(GP, 2 * GP), False)
                with act.Fori(0, FC - 1) as it:
                    up_groups(f, Place(up + 2 * GP, it, 2 * GP), it + 1, range(2 * GP), True)
                for j in range(GF):
                    if j == GP:
                        hidden_hi(f, FC - 1)
                    split(Place(down), j)
                summed_chunks(down, GF, GP)

            def z_scale(q):
                act.wait_ge(w_used, starts["in"] + GP * (q + 1))
                if q:
                    act.wait_ge(z_xp, q)
                else:
                    act.wait_ge(rstd_pre, 2)
                for t in range(TOK):
                    sc.activation(hid[:, t], bank(2 * (q % 2) + t), ACT.Copy, scale=rstd[:, 1, t:t + 1]
                                  ).then_inc(z_out, 1)

            def z_take(q):
                kind, jc = Z[q]
                if kind in ("x", "b"):
                    return
                act.wait_ge(z_xp, q + 1)
                for h in range(2):
                    src = bank(XP + h).rearrange("p (m q) -> p m q", q=T)
                    dst = slice(2 * h, 2 * h + 2)
                    if kind == "gate":
                        sc.activation(gl[jc][:, dst], src, ACT.Gelu_apprx_tanh).then_inc(z_taken, 1)
                    elif kind == "lru":
                        sc.copy(xpad[:, dst, pad:], src).then_inc(z_taken, 1)
                    else:
                        sc.copy(cc[:, dst], src).then_inc(z_taken, 1)

            def gates(jc, ms):
                if jc:
                    act.wait_ge(y_ready, jc)
                for m in ms:
                    hd = jc * MC + m
                    act.wait_ge(head_mm, hd + 1)
                    sc.activation(rr[:, m], bank(HD + m % 2, T), ACT.Sigmoid, bias=cst[:, B_R + hd:B_R + hd + 1])
                    sc.activation(ii[:, m], bank(HD + m % 2, T, T), ACT.Sigmoid,
                                  bias=cst[:, B_I + hd:B_I + hd + 1]).then_inc(head_sig, 1)
                for m in ms:
                    hd = jc * MC + m
                    act.wait_ge(head_sig, hd + 1)
                    sc.activation(rr[:, m], rr[:, m], ACT.Tanh, scale=sp4[:, hd:hd + 1]).then_inc(tanh_done, 1)
                if m == MC - 1:
                    act.wait_ge(tanh_done, MC * (jc + 1))
                    sc.activation(bb[:], rr[:], ACT.Sqrt).then_inc(sqrt_done, 1)

            GATES = {(Z.index(("lru", jc)) + 3, j): (jc, ms) for jc in range(JC) for j, ms in ((3, (0, 1)), (7, (2, 3)))}

            def mixer_steps(q, j):
                if (q, j) in Z_TAKE:
                    z_take(Z_TAKE[q, j])
                if (q, j) in Z_SCALE:
                    z_scale(Z_SCALE[q, j])
                if (q, j) in GATES:
                    gates(*GATES[q, j])
                if (q, j) in Y_PART:
                    n = Y_PART[q, j]
                    act.wait_ge(y_ready, n + 1)
                    sc.copy(hT_hi[:, MC * n:MC * n + MC, :], yy[:]).then_inc(y_hi, 1)

            ffn(0)
            hand_over(1)
            for q in range(1, NZ):
                for j in range(GP):
                    mixer_steps(q, j)
                    split(Place(starts["in"] + GP * q), j)
            for j in range(GP):
                mixer_steps(NZ, j)
                split(Place(starts["out"]), j)
            summed_chunks(starts["out"], GP, 3)
            ffn(1)
            last_square(2, 0)
            last_square(2, 1)

        @block.vector
        def _(dve):
            ve = nc.vector
            steps = [0]

            def chain(ins):
                steps[0] += 1
                ins.then_inc(step, 1)
                dve.wait_ge(step, steps[0])

            def split(pl, j):
                s = pl.slot(j)
                dve.wait_ge(hi_ready, pl.count(j))
                ve.tensor_tensor(w_lo[:, s], raw[:, s], w_hi[:, s].bitcast(f32), ALU.subtract
                                 ).then_inc(lo_ready, 1)

            def gain_bank(d, n, t):
                dve.wait_ge(sq_done, n * TOK + (TOK * NC * d + t + 1))
                dve.wait_ge(gpost_in, 16 * (d + 1))
                ve.tensor_tensor(bank(n * 2 + t), bank(n * 2 + t), gpost[:, columns(n)], ALU.mult
                                 ).then_inc(fg_done, 1)

            def post_norm(d, t):
                k = 1 if d == 1 else 4
                dve.wait_ge(sq_done, TOK * NC * d + TOK * (NC - 1) + t + 1)
                ve.reduce_sum(tot[:, 0, t:t + 1], sums[:, 0, t], axis=AX.X).then_inc(tot_post, 1)
                dve.wait_ge(tot_post, TOK * d + t + 1)
                ve.tensor_scalar(mean[:, 0, t:t + 1], tot[:, 0, t:t + 1], k / D, k * EPS, ALU.mult, ALU.add
                                 ).then_inc(mean_post, 1)

            def update(d, n, t, c):
                dve.wait_ge(rstd_post, TOK * d + t + 1)
                dve.wait_ge(fg_done, TOK * NC * d + TOK * c + t + 1)
                ve.scalar_tensor_tensor(out=resid[:, t, columns(c)], in0=bank(2 * c + t),
                                        scalar=rstd[:, 0, t:t + 1], in1=resid[:, t, columns(c)],
                                        op0=ALU.mult, op1=ALU.add).then_inc(resid_new, 1)

            def block_gain(r, k):
                t, c = BLOCKS[k]
                dve.wait_ge(blk_xp, NBLK * r + k + 1)
                if k or r:
                    dve.wait_ge(blk_lo, NBLK * r + k)
                a = r * KD + MC * c
                ve.tensor_tensor(gained[:], bank(2 * c + t).rearrange("p (m q) -> p m q", q=P),
                                 cst[:, a:a + MC].unsqueeze(2).broadcast_to([P, MC, P]), ALU.mult
                                 ).then_inc(blk_gain, 1)

            def block_lo(r, k):
                t, c = BLOCKS[k]
                dve.wait_ge(blk_hi, NBLK * r + k + 1)
                ve.tensor_tensor(xT_lo[:, MC * c:MC * c + MC, part(t)], gained[:],
                                 xT_hi[:, MC * c:MC * c + MC, part(t)].bitcast(f32), ALU.subtract
                                 ).then_inc(blk_lo, 1)

            def hand_over(r):
                pl = Place(starts[PHASE[r]])
                for what, n in (("post", 0), ("update", 0), ("split", 0), ("gain", 0), ("update", 1), ("lo", 0),
                                ("split", 1), ("gain", 1), ("split", 2), ("lo", 1), ("post", 1), ("split", 3),
                                ("update", 2), ("gain", 2), ("update", 3), ("lo", 2), ("gain", 3), ("bank", 0),
                                ("update", 4), ("lo", 3), ("gain", 4), ("update", 5), ("lo", 4), ("split", 4),
                                ("gain", 5), ("split", 5), ("bank", 1), ("update", 6), ("lo", 5), ("split", 6),
                                ("gain", 6), ("update", 7), ("lo", 6), ("split", 7), ("gain", 7), ("lo", 7)):
                    if what == "split":
                        split(pl, n)
                    elif what == "gain":
                        block_gain(r, n)
                    elif what == "lo":
                        block_lo(r, n)
                    elif r and what == "post":
                        post_norm(r - 1, n)
                    elif r and what == "bank":
                        gain_bank(r - 1, NC - 1, n)
                    elif r and what == "update":
                        update(r - 1, n, *BLOCKS[n])
                dve.wait_ge(blk_sq, NBLK * (r + 1))
                ve.reduce_sum(tot[:, 1, :], sums[:, 1], axis=AX.X).then_inc(tot_pre, 1)
                dve.wait_ge(tot_pre, r + 1)
                ve.tensor_scalar(mean[:, 1, :], tot[:, 1, :], 1 / D, EPS, ALU.mult, ALU.add).then_inc(mean_pre, 1)

            def hidden(f, c, summed):
                dve.wait_ge(w_used, summed)
                dve.wait_ge(silu_done, c * TOK + (f * FC * TOK + TOK))
                for t in range(TOK):
                    ve.scalar_tensor_tensor(out=hid[:, t], in0=bank(2 + t), scalar=rstd[:, 1, t:t + 1],
                                            in1=act_g[:, t], op0=ALU.mult, op1=ALU.mult).then_inc(hid_done, 1)

            def hidden_lo(f, c):
                tiles = slice(c * MC, c * MC + MC) if isinstance(c, int) else ds(c * MC, MC)
                for t in range(TOK):
                    dve.wait_ge(hT_hi_done, c * TOK + (f * FC * TOK + t + 1))
                    ve.tensor_tensor(hT_lo[:, tiles, part(t)], bank(XP + t).rearrange("p (m q) -> p m q", q=P),
                                     hT_hi[:, tiles, part(t)].bitcast(f32), ALU.subtract).then_inc(hT_lo_done, 1)

            def up_groups(f, pl, c, js, tail):
                for j in js:
                    if tail and j == 3:
                        hidden(f, c - 1, pl.count(-1))
                    if tail and j == GP:
                        hidden_lo(f, c - 1)
                    split(pl, j)

            def summed_chunks(d, g0, n_groups, hook):
                with dve.Fori(0, NC - 1) as it:
                    for j in range(n_groups):
                        if j == hook:
                            for t in range(TOK):
                                gain_bank(d, it, t)
                        split(Place(g0 + n_groups, it, n_groups), j)

            def ffn(f):
                up, down = starts[f"up{f + 1}"], starts[f"down{f + 1}"]
                hand_over(2 * f)
                if f == 0:
                    softplus(Place(up))
                up_groups(f, Place(up), 0, range(GP if f else GP + 4, 2 * GP), False)
                with dve.Fori(0, FC - 1) as it:
                    up_groups(f, Place(up + 2 * GP, it, 2 * GP), it + 1, range(2 * GP), True)
                for j in range(GF):
                    if j == 3:
                        hidden(f, FC - 1, down)
                    if j == GP:
                        hidden_lo(f, FC - 1)
                    split(Place(down), j)
                summed_chunks(2 * f, down, GF, GP + 2)

            def softplus(pl):
                dve.wait_ge(small_xp, 2)
                ve.tensor_copy(cst[:, KD:], bank(7, NB)).then_inc(cst_ready, 1)
                dve.wait_ge(cst_ready, 2)
                lam_t = cst[:, LAM:LAM + HEADS]
                chain(ve.tensor_scalar(soft[:, 2], lam_t, -1.0, None, ALU.mult))
                ve.tensor_tensor(soft[:, 0], lam_t, soft[:, 2], ALU.min).then_inc(lam_neg, 1)
                for j in range(GP, GP + 4):
                    split(pl, j)
                dve.wait_ge(lam_sig, 1)
                q, w, w2 = soft[:, 1], soft[:, 3], soft[:, 4]
                chain(ve.tensor_scalar(w, q, -1.0, 2.0, ALU.mult, ALU.add))
                chain(ve.reciprocal(w, w))
                chain(ve.tensor_tensor(w, w, q, ALU.mult))
                chain(ve.tensor_tensor(w2, w, w, ALU.mult))
                s = soft[:, 0]
                chain(ve.tensor_scalar(s, w2, 1 / 17, None, ALU.mult))
                for k in range(7, 0, -1):
                    chain(ve.scalar_tensor_tensor(out=s, in0=s, scalar=1 / (2 * k + 1), in1=w2,
                                                  op0=ALU.add, op1=ALU.mult))
                chain(ve.scalar_tensor_tensor(out=s, in0=s, scalar=1.0, in1=w, op0=ALU.add, op1=ALU.mult))
                chain(ve.tensor_scalar(soft[:, 2], soft[:, 2], 0.0, 4.0, ALU.max, ALU.mult))
                chain(ve.scalar_tensor_tensor(out=sp4[:], in0=s, scalar=8.0, in1=soft[:, 2],
                                              op0=ALU.mult, op1=ALU.add))

            def conv(dst, m, first_col, taps, weights, bias, done=None):
                for k in range(taps):
                    src = xpad[:, m, first_col + k:first_col + k + T]
                    wk = cst[:, weights + HEADS * k:weights + HEADS * k + 1]
                    if k == 0 and bias is not None:
                        ins = ve.tensor_scalar(dst[:, m], src, wk, bias, ALU.mult, ALU.add)
                    elif k == 0:
                        ins = ve.tensor_scalar(dst[:, m], src, wk, None, ALU.mult)
                    else:
                        ins = ve.scalar_tensor_tensor(out=dst[:, m], in0=src, scalar=wk, in1=dst[:, m],
                                                      op0=ALU.mult, op1=ALU.add)
                    if k == taps - 1 and done is not None:
                        ins.then_inc(done, 1)
                    else:
                        chain(ins)

            def lru_conv(jc, m):
                hd = jc * MC + m
                dve.wait_ge(z_taken, 2 * Z.index(("lru", jc)) + 2)
                if jc:
                    dve.wait_ge(head_mm, MC * jc)
                conv(xc, m, 0, TAPS_A, CONV_W + hd, cst[:, CONV_B + hd:CONV_B + hd + 1], xc_ready)

            def lru(jc, what):
                if what[0] == "r":
                    m = int(what[1])
                    dve.wait_ge(tanh_done, jc * MC + m + 1)
                    chain(ve.tensor_scalar(aa[:, m], rr[:, m], 1.0, None, ALU.add))
                    chain(ve.reciprocal(aa[:, m], aa[:, m]))
                elif what == "ix":
                    dve.wait_ge(head_sig, jc * MC + MC)
                    chain(ve.tensor_tensor(ii[:], ii[:], xc[:], ALU.mult))
                elif what == "b":
                    dve.wait_ge(sqrt_done, jc + 1)
                    chain(ve.scalar_tensor_tensor(out=bb[:], in0=bb[:], scalar=2.0, in1=aa[:],
                                                  op0=ALU.mult, op1=ALU.mult))
                    chain(ve.tensor_tensor(bb[:], bb[:], ii[:], ALU.mult))
                elif what[0] == "s":
                    if what == "s0":
                        chain(ve.tensor_scalar(aa[:], aa[:], 2.0, -1.0, ALU.mult, ALU.add))
                    for m in (int(what[1]), int(what[1]) + 1):
                        chain(ve.tensor_tensor_scan(out=yc[:, m], data0=aa[:, m], data1=bb[:, m], initial=0.0,
                                                    op0=ALU.mult, op1=ALU.add))
                else:
                    if jc:
                        dve.wait_ge(y_lo, jc)
                    ve.tensor_tensor(yy[:], yc[:], gl[jc][:], ALU.mult).then_inc(y_ready, 1)

            def z_take(q):
                kind, jc = Z[q]
                if kind not in ("x", "b"):
                    return
                dve.wait_ge(z_xp, q + 1)
                if kind == "x":
                    dve.wait_ge(z_taken, 2 * q)
                elif kind == "b":
                    dve.wait_ge(y_lo, 2 + jc)
                for h in range(2):
                    src = bank(XP + h).rearrange("p (m q) -> p m q", q=T)
                    dst = slice(2 * h, 2 * h + 2)
                    if kind == "x":
                        ve.tensor_tensor(xpad[:, dst, pad:], src, cc[:, dst], ALU.mult).then_inc(z_taken, 1)
                    else:
                        ve.tensor_tensor(yy[:, dst], src, yc[:, dst], ALU.mult).then_inc(z_taken, 1)
                if kind == "b":
                    dve.wait_ge(z_taken, 2 * q + 2)
                    dve.sem_inc(y_ready, 1)

            def short_conv(jc, m):
                ft = jc * MC + m
                dve.wait_ge(z_taken, 2 * Z.index(("x", jc)) + 2)
                dve.wait_ge(y_ready, 2 + jc)
                conv(yc, m, pad + 1 - TAPS_B, TAPS_B, SC_W + ft, None)

            LRU_CONV = {(Z.index(("lru", jc)) + 2, 1 + m): (jc, m) for jc in range(JC) for m in range(MC)}
            LRU = {(4, 4): (0, "r0"), (4, 5): (0, "r1"), (5, 0): (0, "ix"), (5, 5): (0, "r2"), (5, 6): (0, "r3"),
                   (5, 7): (0, "b"), (6, 0): (0, "s0"), (6, 1): (0, "s2"), (6, 2): (0, "y"),
                   (6, 4): (1, "r0"), (6, 5): (1, "r1"), (7, 0): (1, "ix"), (7, 1): (1, "r2"), (7, 2): (1, "r3"),
                   (7, 3): (1, "b"), (7, 4): (1, "s0"), (7, 5): (1, "s2"), (7, 6): (1, "y")}
            SHORT = {(7, 7): ((0, 0),), (8, 0): ((0, 1),), (8, 1): ((0, 2),), (8, 2): ((0, 3),),
                     (NZ, 0): ((1, 0),), (NZ, 1): ((1, 1),), (NZ, 2): ((1, 2),), (NZ, 3): ((1, 3),)}

            def mixer_steps(q, j):
                if (q, j) in Z_TAKE:
                    z_take(Z_TAKE[q, j])
                if (q, j) in LRU:
                    lru(*LRU[q, j])
                if (q, j) in LRU_CONV:
                    lru_conv(*LRU_CONV[q, j])
                for jc, m in SHORT.get((q, j), ()):
                    short_conv(jc, m)
                if (q, j) in Y_PART:
                    n = Y_PART[q, j]
                    dve.wait_ge(y_hi, n + 1)
                    ve.tensor_tensor(hT_lo[:, MC * n:MC * n + MC, :], yy[:],
                                     hT_hi[:, MC * n:MC * n + MC, :].bitcast(f32), ALU.subtract).then_inc(y_lo, 1)

            dve.wait_ge(small_xp, 1)
            ve.tensor_copy(cst[:, 0:KD], bank(6, KD)).then_inc(cst_ready, 1)
            dve.wait_ge(cst_ready, 1)

            ffn(0)
            hand_over(1)
            for q in range(1, NZ):
                for j in range(GP):
                    mixer_steps(q, j)
                    split(Place(starts["in"] + GP * q), j)
            for j in range(GP):
                mixer_steps(NZ, j)
                split(Place(starts["out"]), j)
            summed_chunks(1, starts["out"], GP, 5)
            ffn(1)
            for t in range(TOK):
                post_norm(2, t)
                gain_bank(2, NC - 1, t)
                for c in range(NC):
                    update(2, NC * t + c, t, c)

        @block.tensor
        def _(pe):
            te = nc.tensor

            def products(pl, j, hi, lo, kt, t, dst, start, stop):
                s = pl.slot(j)
                for k in range(GK):
                    xh, xl = hi[:, kt + k, part(t)], lo[:, kt + k, part(t)]
                    te.matmul(dst, xh, w_hi[:, s, k], start=start and k == 0, stop=False)
                    te.matmul(dst, xh, w_lo[:, s, k], start=False, stop=False)
                    last = te.matmul(dst, xl, w_hi[:, s, k], start=False, stop=stop and k == GK - 1)
                return last

            def group(pl, j, hi, lo, jk, n_groups, banks):
                pe.wait_ge(lo_ready, pl.count(j))
                for t in range(TOK):
                    last = products(pl, j, hi, lo, GK * jk, t, banks[t], jk == 0, jk == n_groups - 1)
                last.then_inc(w_used, 1)

            def last_groups(pl, j0, hi, lo, n_groups, banks, at_group=None, r=None):
                for t in range(TOK):
                    for j in range(j0, n_groups):
                        if r and t == 1 and j == j0 + 2:
                            block_transpose(r, 0)
                        if t == 0:
                            if at_group:
                                at_group(j)
                            pe.wait_ge(lo_ready, pl.count(j))
                        last = products(pl, j, hi, lo, GK * j, t, banks[t], j == 0, j == n_groups - 1)
                        if t == TOK - 1:
                            last.then_inc(w_used, 1)
                    if t == 0:
                        last.then_inc(tok0_done, 1)

            def block_transpose(r, k):
                t, c = BLOCKS[k]
                if r:
                    pe.wait_ge(resid_new, NBLK * (r - 1) + k + 1)
                else:
                    pe.wait_ge(x_in[2 * t + c // 2], 16)
                for m in range(MC):
                    last = te.transpose(bank(2 * c + t, P, m * P), resid[:, t, c * W + m * P:c * W + m * P + P],
                                        ident[:])
                last.then_inc(blk_xp, 1)

            def first_chunk(r):
                pl = Place(starts[PHASE[r]])

                def mm(k, h):
                    t, c = BLOCKS[k]
                    j = 2 * c + h
                    pe.wait_ge(lo_ready, pl.count(j))
                    pe.wait_ge(blk_lo, NBLK * r + k + 1)
                    last = products(pl, j, xT_hi, xT_lo, GK * j, t, bank(t), j == 0, j == GP - 1)
                    if t == TOK - 1:
                        last.then_inc(w_used, 1)

                if not r:
                    block_transpose(r, 0)
                block_transpose(r, 1)
                mm(0, 0)
                mm(0, 1)
                mm(1, 0)
                mm(1, 1)
                block_transpose(r, 2)
                block_transpose(r, 3)
                for k in range(2, NBLK):
                    mm(k, 0)
                    if k + 2 < NBLK:
                        block_transpose(r, k + 2)
                    mm(k, 1)

            def summed_chunks(g0, n_groups, r):
                def chunk(pl, n, r=None):
                    banks = (bank(n * 2), bank(n * 2 + 1))
                    for j in range(n_groups - 4):
                        group(pl, j, hT_hi, hT_lo, j, n_groups, banks)
                    last_groups(pl, n_groups - 4, hT_hi, hT_lo, n_groups, banks, r=r)

                with pe.Fori(0, NC - 2) as it:
                    chunk(Place(g0 + n_groups, it, n_groups), it + 1)
                chunk(Place(g0 + (NC - 1) * n_groups), NC - 1, r)

            def hidden_transpose(f, c):
                for t in range(TOK):
                    pe.wait_ge(hid_done, c * TOK + (f * FC * TOK + t + 1))
                    for m in range(MC):
                        last = te.transpose(bank(XP + t, P, m * P), hid[:, t, m * P:m * P + P], ident[:])
                    last.then_inc(hid_xp, 1)

            def ffn(f):
                up, down = starts[f"up{f + 1}"], starts[f"down{f + 1}"]
                done = f * FC * TOK
                first_chunk(2 * f)
                if f == 0:
                    pe.wait_ge(small_b_in, 16 * 8)
                    te.transpose(bank(7, NB), small_b[:], ident[0:NB, 0:NB]).then_inc(small_xp, 1)
                for j in range(GP):
                    group(Place(up + GP), j, xT_hi, xT_lo, j, GP, (bank(2), bank(3)))
                with pe.Fori(0, FC - 1) as it:
                    pl = Place(up + 2 * GP, it, 2 * GP)
                    pe.wait_ge(silu_done, it * TOK + (done + TOK))
                    for j in range(GP):
                        group(pl, j, xT_hi, xT_lo, j, GP, (bank(0), bank(1)))
                        if j == 3:
                            hidden_transpose(f, it)
                    pe.wait_ge(hid_done, it * TOK + (done + TOK))
                    for j in range(GP):
                        group(pl, GP + j, xT_hi, xT_lo, j, GP, (bank(2), bank(3)))
                pe.wait_ge(silu_done, done + FC * TOK)
                pe.wait_ge(hT_lo_done, done + (FC - 1) * TOK)
                pl = Place(down)
                for j in range(GF - 4):
                    group(pl, j, hT_hi, hT_lo, j, GF, (bank(0), bank(1)))
                    if j == 3:
                        hidden_transpose(f, FC - 1)
                pe.wait_ge(hT_lo_done, done + FC * TOK)
                last_groups(pl, GF - 4, hT_hi, hT_lo, GF, (bank(0), bank(1)))
                pe.wait_ge(hid_done, done + FC * TOK)
                summed_chunks(down, GF, None if f else 1)

            def z_transpose(q):
                pe.wait_ge(z_out, TOK * (q + 1))
                if q:
                    pe.wait_ge(z_taken, 2 * q)
                for t in range(TOK):
                    for m in range(MC):
                        last = te.transpose(bank(XP + m // 2, P, (m % 2) * T + t * P),
                                            hid[:, t, m * P:m * P + P], ident[:])
                last.then_inc(z_xp, 1)

            def head_products(jc, ms):
                for m in ms:
                    hd = jc * MC + m
                    pe.wait_ge(xc_ready, hd + 1)
                    pe.wait_ge(heads_in, 32)
                    if hd >= 2:
                        pe.wait_ge(head_sig, hd - 1)
                    for n in range(2):
                        last = te.matmul(bank(HD + m % 2, T, n * T), w_ri[:, n, hd], xc[:, m],
                                         start=True, stop=True)
                    last.then_inc(head_mm, 1)

            HEADS_AT = {(Z.index(("lru", jc)) + dq, j): (jc, ms) for jc in range(JC)
                        for dq, j, ms in ((2, 6, (0, 1)), (3, 3, (2, 3)))}

            pe.wait_ge(pool_set, 3)
            pe.wait_ge(small_a_in, 16)
            te.transpose(bank(6, KD), small_a[:], ident[0:KD, 0:KD]).then_inc(small_xp, 1)
            pe.wait_ge(cst_ready, 1)

            ffn(0)
            first_chunk(1)
            for q in range(1, NZ):
                pl = Place(starts["in"] + GP * q)
                if q > 1:
                    pe.wait_ge(z_out, TOK * (q - 1))
                for j in range(GP):
                    group(pl, j, xT_hi, xT_lo, j, GP, (bank(2 * (q % 2)), bank(2 * (q % 2) + 1)))
                    if j == 3:
                        z_transpose(q - 1)
                    if (q, j) in HEADS_AT:
                        head_products(*HEADS_AT[q, j])
            pl = Place(starts["out"])
            pe.wait_ge(z_out, TOK * (NZ - 1))
            for j in range(4):
                if j % 2 == 0:
                    pe.wait_ge(y_lo, j // 2 + 1)
                group(pl, j, hT_hi, hT_lo, j, GP, (bank(0), bank(1)))
                if j == 1:
                    z_transpose(NZ - 1)

            def y_part(j):
                if j % 2 == 0:
                    pe.wait_ge(y_lo, j // 2 + 1)
            last_groups(pl, 4, hT_hi, hT_lo, GP, (bank(0), bank(1)), y_part)
            pe.wait_ge(head_sig, HEADS)
            summed_chunks(starts["out"], GP, 2)
            ffn(1)


_INS = ["x", "ffn1_pre_g", "ffn1_w_gate", "ffn1_w_up", "ffn1_w_down", "ffn1_post_g", "mix_pre_g", "w_in",
        "lru_conv_w", "lru_conv_b", "lru_w_r", "lru_b_r", "lru_w_i", "lru_b_i", "lru_lambda", "sc_conv_w",
        "w_out", "mix_post_g", "ffn2_pre_g", "ffn2_w_gate", "ffn2_w_up", "ffn2_w_down", "ffn2_post_g"]


def kernel(**inputs):
    import numpy as _np
    import concourse.bacc as _bacc
    from concourse import mybir as _mybir
    from concourse.bass_utils import run_bass_kernel_spmd as _run

    nc = _bacc.Bacc("TRN2", target_bir_lowering=False, num_devices=1)
    arrays, args = {}, []
    for name in _INS:
        a = _np.ascontiguousarray(inputs[name])
        arrays[f"in_{name}"] = a
        args.append(nc.dram_tensor(f"in_{name}", a.shape, _mybir.dt.from_np(a.dtype), kind="ExternalInput").ap())
    shape = tuple(inputs["x"].shape)
    args.append(nc.dram_tensor("out_0", shape, _mybir.dt.float32, kind="ExternalOutput").ap())
    hybrid_block_kernel(nc, *args)
    r = _run(nc, [arrays], core_ids=[0])
    return r.results[0]["out_0"]
```

```python
import concourse.bass as bass
from concourse import mybir
from contextlib import ExitStack


P = 128
TOK = 2
W = 512
GK = 2
SLOTS = 4
EPS = 1e-6


def hybrid_block_kernel(nc, x, f1_pre, f1_wg, f1_wu, f1_wd, f1_post, mix_pre, w_in, conv_w, conv_b,
                        w_r, b_r, w_i, b_i, lam, sc_w, w_out, mix_post, f2_pre, f2_wg, f2_wu, f2_wd,
                        f2_post, out):
    f32, f32r = mybir.dt.float32, mybir.dt.float32r
    ALU, ACT, AX = mybir.AluOpType, mybir.ActivationFunctionType, mybir.AxisListType
    ds = bass.ds

    D, F = f1_wg.shape[1], f1_wg.shape[2]
    DIN = w_in.shape[2]
    DL = lam.shape[1]
    HEADS = w_r.shape[1]
    TAPS_A, TAPS_B = conv_w.shape[1], sc_w.shape[1]
    T = TOK * P
    KD, KF = D // P, F // P
    MC = W // P
    NC = D // W
    FC = F // W
    JC = DL // W
    GP, GF = KD // GK, KF // GK
    assert x.shape == (1, T, D) and DIN == 5 * DL and 2 * DL == D and JC == 2 and HEADS == DL // P
    assert GP == 2 * SLOTS and GF == 22 and NC == 4

    four = [j % SLOTS for j in range(GP)]
    short = 2 * (SLOTS - 1)
    odd = [j % (SLOTS - 1) for j in range(short)] + [j % SLOTS for j in range(GF - short)]
    slots, starts = [], {}
    for name, n, pattern in (("up1", 2 * FC, four), ("down1", NC, odd), ("in", 5 * JC, four),
                             ("out", NC, four), ("up2", 2 * FC, four), ("down2", NC, odd)):
        starts[name] = len(slots)
        slots += pattern * n
    starts["end"] = len(slots)
    before, uses, last_use, count = [], [], [None] * SLOTS, [0] * SLOTS
    for g, s in enumerate(slots):
        before.append(last_use[s])
        count[s] += 1
        uses.append(count[s])
        last_use[s] = g

    class Place:

        def __init__(self, g0, it=0, stride=0):
            self.g0, self.it, self.stride = g0, it, stride

        def slot(self, j):
            return slots[self.g0 + j]

        def count(self, j):
            return self.it * self.stride + (self.g0 + j + 1)

        def first(self, j):
            return before[self.g0 + j] is None

        def freed(self, j):
            return self.it * self.stride + (before[self.g0 + j] + 1)

        def loaded(self, j):
            g = self.g0 + j
            per = 16 * (uses[g + self.stride] - uses[g]) if self.stride else 0
            return self.it * per + 16 * uses[g]

    def rows(w):
        return w[0].rearrange("(k p) n -> p k n", p=P)

    ffn_w = {0: (rows(f1_wg), rows(f1_wu), rows(f1_wd)), 1: (rows(f2_wg), rows(f2_wu), rows(f2_wd))}
    w_in_v, w_out_v = rows(w_in), rows(w_out)
    x_v, out_v = rows(x), rows(out)

    ctx = ExitStack()
    with ctx:
        def sb(name, shape, dt=f32):
            return ctx.enter_context(nc.sbuf_tensor(name, shape, dt))

        def sem(name):
            return ctx.enter_context(nc.semaphore(name))

        raw = sb("raw", [P, SLOTS, GK, W])
        w_hi = sb("w_hi", [P, SLOTS, GK, W], f32r)
        w_lo = sb("w_lo", [P, SLOTS, GK, W], f32r)
        xT_hi = sb("xT_hi", [P, KD, T], f32r)
        xT_lo = sb("xT_lo", [P, KD, T], f32r)
        resid = sb("resid", [P, TOK, D])
        gpost = sb("gpost", [P, D])
        act_g = sb("act_g", [P, TOK, W])
        hid = sb("hid", [P, TOK, W])
        ident = sb("ident", [P, P])
        NB = 2 * KD + (TAPS_A + 4 + TAPS_B) * HEADS
        small_a = sb("small_a", [KD, P])
        small_b = sb("small_b", [NB, P])
        cst = sb("cst", [P, KD + NB])
        sums = sb("sums", [P, 2, TOK, NC])
        tot = sb("tot", [P, 2, TOK])
        mean = sb("mean", [P, 2, TOK])
        rstd = sb("rstd", [P, 2, TOK])
        power = sb("power", [P, TOK])
        soft = sb("soft", [P, 5, HEADS])
        sp4 = sb("sp4", [P, HEADS])
        sp8n = sb("sp8n", [P, HEADS])

        region_at = (nc.sbuf_base + 31) // 32 * 32
        region_size = 4 * 2 * KF * T
        sb("region", [P, 2 * KF * T])

        def at(name, shape, offset, dt=f32):
            size = 4
            for n in shape[1:]:
                size *= n
            assert offset + size <= region_size
            return nc.alloc_sbuf_tensor_at(name, shape, dt, offset=region_at + offset), offset + size

        hT_hi, o = at("hT_hi", [P, KF, T], 0, f32r)
        hT_lo, o = at("hT_lo", [P, KF, T], o, f32r)
        o = 4 * KD * T
        pad = TAPS_A - 1
        xc, o = at("xc", [P, MC, T], o)
        rr, o = at("rr", [P, MC, T], o)
        ii, o = at("ii", [P, MC, T], o)
        gl0, o = at("gl0", [P, MC, T], o)
        gl1, o = at("gl1", [P, MC, T], o)
        xpad, o = at("xpad", [P, MC, pad + T], o)
        assert o <= 4 * KF * T
        o = 4 * KF * T + 4 * KD * T
        aa, o = at("aa", [P, MC, T], o)
        bb, o = at("bb", [P, MC, T], o)
        cc, o = at("cc", [P, MC, T], o)
        yc, o = at("yc", [P, MC, T], o)
        yy, o = at("yy", [P, MC, T], o)
        w_ri, o = at("w_ri", [P, 2, HEADS, P], o)
        gl = (gl0, gl1)

        ps = ctx.enter_context(nc.psum_tensor("ps", [P, 8 * W], f32))
        XP, HD = 4, 6

        def bank(n, width=W, start=0):
            if isinstance(n, int):
                return ps[:, n * W + start:n * W + start + width]
            return ps[:, ds(n * W + start, width)]

        def columns(n, width=W):
            return slice(n * width, n * width + width) if isinstance(n, int) else ds(n * width, width)

        def part(t):
            return slice(t * P, t * P + P)

        raw_full = [sem(f"raw_full{s}") for s in range(SLOTS)]
        hi_ready = sem("hi_ready")
        lo_ready = sem("lo_ready")
        w_used = sem("w_used")
        tok0_done = sem("tok0_done")
        x_in = [sem(f"x_in{k}") for k in range(TOK * NC)]
        table_in = sem("table_in")
        small_a_in, small_b_in = sem("small_a_in"), sem("small_b_in")
        heads_in, gpost_in = sem("heads_in"), sem("gpost_in")
        pool_set = sem("pool_set")
        pads_set = sem("pads_set")
        small_xp = sem("small_xp")
        cst_ready = sem("cst_ready")
        sq_done = sem("sq_done")
        fg_done = sem("fg_done")
        tot_post, mean_post = sem("tot_post"), sem("mean_post")
        rstd_post = sem("rstd_post")
        resid_new = sem("resid_new")
        blk_xp = sem("blk_xp")
        blk_hi = sem("blk_hi")
        blk_lo = sem("blk_lo")
        blk_sq = sem("blk_sq")
        tot_pre, mean_pre = sem("tot_pre"), sem("mean_pre")
        rstd_pre = sem("rstd_pre")
        silu_done = sem("silu_done")
        hid_done = sem("hid_done")
        hid_xp = sem("hid_xp")
        hT_hi_done = sem("hT_hi_done")
        hT_lo_done = sem("hT_lo_done")
        z_out = sem("z_out")
        z_xp = sem("z_xp")
        z_taken = sem("z_taken")
        step = sem("step")
        lam_neg = sem("lam_neg")
        lam_sig = sem("lam_sig")
        xc_ready = sem("xc_ready")
        head_mm = sem("head_mm")
        head_sig = sem("head_sig")
        tanh_done = sem("tanh_done")
        a_done = sem("a_done")
        sqrt_done = sem("sqrt_done")
        y_ready = sem("y_ready")
        y_hi = sem("y_hi")
        y_lo = sem("y_lo")
        stored = sem("stored")

        BLOCKS = [(0, 0), (0, 1), (1, 0), (1, 1), (0, 2), (0, 3), (1, 2), (1, 3)]
        NBLK = len(BLOCKS)
        CONV_W, CONV_B, B_R, B_I, LAM, SC_W = (
            3 * KD + HEADS * n for n in (0, TAPS_A, TAPS_A + 1, TAPS_A + 2, TAPS_A + 3, TAPS_A + 4))
        HI_FIRST = ("split:0 hi:0 split:1 hi:1 split:2 split:3 hi:2 hi:3 split:4 hi:4 split:5 hi:5 "
                    "split:6 split:7 hi:6 hi:7")
        LO_FIRST = HI_FIRST.replace("hi", "lo")
        HI = ("square:0 split:0 hi:0 split:1 split:2 square:1 hi:1 split:3 hi:2 hi:3 split:4 hi:4 "
              "split:5 hi:5 split:6 split:7 hi:6 hi:7")
        LO = ("post:0 update:0 update:1 split:0 lo:0 split:1 post:1 split:2 update:2 lo:1 update:3 "
              "lo:2 update:4 lo:3 bank:0 update:5 split:4 lo:4 bank:1 update:6 lo:5 split:6 "
              "update:7 split:7 lo:6 lo:7")
        POOL_SPLITS = ((), (3, 5), (3, 5))

        def order(steps):
            return [(what, int(n)) for what, n in (step.split(":") for step in steps.split())]

        PHASE = ("up1", "in", "up2")
        Z = [(kind, jc) for kinds in (("gate", "lru"), ("c", "x", "b")) for jc in range(JC) for kind in kinds]
        Z_COL = {kind: n * DL for n, kind in enumerate(("lru", "gate", "b", "c", "x"))}
        NZ = len(Z)
        Z_SCALE = {(q + 1, 3 if q else 5): q for q in range(NZ)}
        B0 = Z.index(("b", 0))
        Z_TAKE = {(q + 2, 0): q for q in range(NZ - 1) if q != B0}
        Z_TAKE[B0 + 2, 3], Z_TAKE[NZ, 5] = B0, NZ - 1
        Y_PART = {(6, 6): 0, (8, 0): 1, (8, 5): 2, (NZ, 5): 3}

        block = ctx.enter_context(nc.Block())

        @block.sync
        def _(sync):
            def load(pl, j, src):
                s = pl.slot(j)
                if not pl.first(j):
                    sync.wait_ge(lo_ready, pl.freed(j))
                sync.dma_start(raw[:, s], src).then_inc(raw_full[s], 16)

            def load_gain(g):
                sync.dma_start(gpost[:], g.broadcast_to([P, D])).then_inc(gpost_in, 16)

            def load_small_b():
                row = 0
                for a, n in ((mix_pre[0].rearrange("(k p) -> k p", p=P), KD),
                             (f2_pre[0].rearrange("(k p) -> k p", p=P), KD)):
                    sync.dma_start(small_b[row:row + n, :], a).then_inc(small_b_in, 16)
                    row += n
                for a, n in ((conv_w[0].rearrange("t (k p) -> (t k) p", p=P), TAPS_A),
                             (conv_b[0].rearrange("(k p) -> k p", p=P), 1), (b_r[0], 1), (b_i[0], 1),
                             (lam[0].rearrange("(k p) -> k p", p=P), 1),
                             (sc_w[0].rearrange("t (k p) -> (t k) p", p=P), TAPS_B)):
                    sync.dma_start(small_b[row:row + n * HEADS, :], a).then_inc(small_b_in, 16)
                    row += n * HEADS

            def load_chunk(pl, w, c, js):
                for j in js:
                    load(pl, j, w[:, GK * j:GK * j + GK, columns(c)])

            def ffn(f):
                up, down = starts[f"up{f + 1}"], starts[f"down{f + 1}"]
                w_gate, w_up, w_down = ffn_w[f]
                for j in range(GP):
                    load_chunk(Place(up), w_gate, 0, [j])
                    for k in (X_LOADS[j] if f == 0 else ()):
                        t, c = BLOCKS[k]
                        sync.dma_start(resid[:, t, columns(c)], x_v[:, t, columns(c)]).then_inc(x_in[k], 16)
                if f == 0:
                    load_small_b()
                load_chunk(Place(up + GP), w_up, 0, range(GP))
                if f == 1:
                    sync.wait_ge(fg_done, 2 * TOK * NC)
                load_gain((f1_post, f2_post)[f])
                with sync.Fori(0, FC - 1) as it:
                    load_chunk(Place(up + 2 * GP, it, 2 * GP), w_gate, it + 1, range(GP))
                    load_chunk(Place(up + 3 * GP, it, 2 * GP), w_up, it + 1, range(GP))
                load_chunk(Place(down), w_down, 0, range(GF))
                with sync.Fori(0, NC - 1) as it:
                    load_chunk(Place(down + GF, it, GF), w_down, it + 1, range(GF))

            X_LOADS = ((0, 1), (2,), (3,), (4, 5, 6, 7), (), (), (), ())
            ffn(0)
            for q, (kind, jc) in enumerate(Z):
                if q == 1:
                    sync.wait_ge(fg_done, TOK * NC)
                    load_gain(mix_post)
                    sync.wait_ge(w_used, starts["in"])
                    for m, w in enumerate((w_r, w_i)):
                        sync.dma_start(w_ri[:, m], w[0].rearrange("h d e -> d h e")).then_inc(heads_in, 16)
                load_chunk(Place(starts["in"] + GP * q), w_in_v, Z_COL[kind] // W + jc, range(GP))
            load_chunk(Place(starts["out"]), w_out_v, 0, range(GP))
            with sync.Fori(0, NC - 1) as it:
                load_chunk(Place(starts["out"] + GP, it, GP), w_out_v, it + 1, range(GP))
            ffn(1)
            for n in range(TOK * NC):
                t, c = n // NC, n % NC
                sync.wait_ge(resid_new, 2 * NBLK + n + 1)
                sync.dma_start(out_v[:, t, columns(c)], resid[:, t, columns(c)]).then_inc(stored, 16)
            sync.wait_ge(stored, 16 * TOK * NC)

        @block.gpsimd
        def _(pool):
            pool.memset(power[:], -0.5).then_inc(pool_set, 1)
            pool.memset(ident[:], 0.0).then_inc(pool_set, 1)
            pool.wait_ge(pool_set, 2)
            pool.affine_select(out=ident[:], in_=ident[:], compare_op=ALU.not_equal, fill=1.0, base=0,
                               pattern=[[-1, P]], channel_multiplier=1).then_inc(pool_set, 1)

            def post(d):
                for t in range(TOK):
                    pool.wait_ge(mean_post, TOK * d + t + 1)
                    pool.tensor_tensor(rstd[:, 0, t:t + 1], mean[:, 0, t:t + 1], power[:, 0:1],
                                       ALU.pow).then_inc(rstd_post, 1)

            def splits(r):
                pl = Place(starts[PHASE[r]])
                for j in POOL_SPLITS[r]:
                    pool.wait_ge(hi_ready, pl.count(j))
                    pool.wait_ge(lo_ready, pl.count(j - 1))
                    s = pl.slot(j)
                    pool.tensor_tensor(w_lo[:, s], raw[:, s], w_hi[:, s].bitcast(f32), ALU.subtract
                                       ).then_inc(lo_ready, 1)

            def pre(r):
                pool.wait_ge(mean_pre, r + 1)
                pool.tensor_tensor(rstd[:, 1, :], mean[:, 1, :], power[:], ALU.pow).then_inc(rstd_pre, 1)

            pre(0)
            post(0)
            pool.wait_ge(w_used, starts["in"])
            pool.memset(xpad[:, :, 0:pad], 0.0).then_inc(pads_set, 1)
            splits(1)
            pre(1)
            post(1)
            splits(2)
            pre(2)
            post(2)

        @block.scalar
        def _(act):
            sc = nc.scalar
            act.dma_start(small_a[:], f1_pre[0].rearrange("(k p) -> k p", p=P)).then_inc(small_a_in, 16)
            act.wait_ge(pool_set, 1)
            sc.activation(act_g[:, 0, 0:1], power[:, 0:1], ACT.Copy).then_inc(table_in, 1)
            act.wait_ge(table_in, 1)

            def split(pl, j):
                s = pl.slot(j)
                act.wait_ge(raw_full[s], pl.loaded(j))
                if not pl.first(j):
                    act.wait_ge(w_used, pl.freed(j))
                sc.copy(w_hi[:, s], raw[:, s]).then_inc(hi_ready, 1)

            def bank_square(n, t):
                sc.activation(act_g[:, t], bank(n * 2 + t), ACT.Square,
                              accum_out=sums[:, 0, t, (slice(n, n + 1) if isinstance(n, int) else ds(n, 1))]
                              ).then_inc(sq_done, 1)

            def last_square(d, t):
                if t == 0:
                    act.wait_ge(tok0_done, NC * (d + 1))
                else:
                    act.wait_ge(w_used, starts[("in", "up2", "end")[d]])
                bank_square(NC - 1, t)

            def block_hi(r, k):
                t, c = BLOCKS[k]
                act.wait_ge(blk_xp, NBLK * r + k + 1)
                for m in range(MC):
                    f = MC * c + m
                    ins = sc.activation(xT_hi[:, f, part(t)], bank(2 * c + t, P, m * P), ACT.Copy,
                                        scale=cst[:, r * KD + f:r * KD + f + 1])
                ins.then_inc(blk_hi, 1)

            def block_squares(r, j):
                for k in (2 * j, 2 * j + 1):
                    t, c = BLOCKS[k]
                    if r:
                        act.wait_ge(resid_new, NBLK * (r - 1) + k + 1)
                    if k or r:
                        act.wait_ge(blk_sq, NBLK * r + k)
                    sc.activation(act_g[:, t], resid[:, t, columns(c)], ACT.Square,
                                  accum_out=sums[:, 1, t, c:c + 1]).then_inc(blk_sq, 1)

            def hand_over(r):
                pl = Place(starts[PHASE[r]])
                act.wait_ge(cst_ready, min(r, 1) + 1)
                for what, n in order(HI_FIRST if r == 0 else HI):
                    if what == "split":
                        split(pl, n)
                    elif what == "hi":
                        block_hi(r, n)
                    else:
                        last_square(r - 1, n)

            def hidden_hi(f, c):
                for t in range(TOK):
                    act.wait_ge(hid_xp, c * TOK + (f * FC * TOK + t + 1))
                    sc.copy(hT_hi[:, (slice(c * MC, c * MC + MC) if isinstance(c, int) else ds(c * MC, MC)), part(t)],
                            bank(XP + t).rearrange("p (m q) -> p m q", q=P)).then_inc(hT_hi_done, 1)

            def up_groups(f, pl, c, js, tail):
                for j in js:
                    if tail and j == GP:
                        hidden_hi(f, c - 1)
                    if not tail and j < GP + 4:
                        block_squares(2 * f, j - GP)
                    if not tail and f == 0 and j == GP + 6:
                        act.wait_ge(lam_neg, 1)
                        sc.activation(soft[:, 1], soft[:, 0], ACT.Sigmoid).then_inc(lam_sig, 1)
                    if j == (GP + 3 if tail else GP + 5):
                        act.wait_ge(w_used, pl.count(GP - 1))
                        act.wait_ge(rstd_pre, 1 + 2 * f)
                        if tail or f:
                            act.wait_ge(hid_done, c * TOK + f * FC * TOK)
                        for t in range(TOK):
                            sc.activation(act_g[:, t], bank(t), ACT.Silu, scale=rstd[:, 1, t:t + 1]
                                          ).then_inc(silu_done, 1)
                    split(pl, j)

            def summed_chunks(g0, n_groups, hook):
                with act.Fori(0, NC - 1) as it:
                    pl = Place(g0 + n_groups, it, n_groups)
                    for j in range(n_groups):
                        if j == hook:
                            act.wait_ge(w_used, pl.count(-1))
                            for t in range(TOK):
                                bank_square(it, t)
                        split(pl, j)

            def ffn(f):
                up, down = starts[f"up{f + 1}"], starts[f"down{f + 1}"]
                hand_over(2 * f)
                up_groups(f, Place(up), 0, range(GP, 2 * GP), False)
                with act.Fori(0, FC - 1) as it:
                    up_groups(f, Place(up + 2 * GP, it, 2 * GP), it + 1, range(2 * GP), True)
                for j in range(GF):
                    if j == GP:
                        hidden_hi(f, FC - 1)
                    split(Place(down), j)
                summed_chunks(down, GF, GP)

            def z_scale(q):
                act.wait_ge(w_used, starts["in"] + GP * (q + 1))
                if q:
                    act.wait_ge(z_xp, q)
                else:
                    act.wait_ge(rstd_pre, 2)
                for t in range(TOK):
                    sc.activation(hid[:, t], bank(2 * (q % 2) + t), ACT.Copy, scale=rstd[:, 1, t:t + 1]
                                  ).then_inc(z_out, 1)

            def z_take(q):
                kind, jc = Z[q]
                if kind in ("x", "b"):
                    return
                act.wait_ge(z_xp, q + 1)
                for h in range(2):
                    src = bank(XP + h).rearrange("p (m q) -> p m q", q=T)
                    dst = slice(2 * h, 2 * h + 2)
                    if kind == "gate":
                        sc.activation(gl[jc][:, dst], src, ACT.Gelu_apprx_tanh).then_inc(z_taken, 1)
                    elif kind == "lru":
                        sc.copy(xpad[:, dst, pad:], src).then_inc(z_taken, 1)
                    else:
                        sc.copy(cc[:, dst], src).then_inc(z_taken, 1)

            def gates(jc, what, ms):
                for m in ms:
                    hd = jc * MC + m
                    if what == "sigmoid":
                        if jc:
                            act.wait_ge(y_ready, jc)
                        act.wait_ge(head_mm, hd + 1)
                        sc.activation(rr[:, m], bank(HD + m % 2, T), ACT.Sigmoid, bias=cst[:, B_R + hd:B_R + hd + 1])
                        sc.activation(ii[:, m], bank(HD + m % 2, T, T), ACT.Sigmoid,
                                      bias=cst[:, B_I + hd:B_I + hd + 1]).then_inc(head_sig, 1)
                    elif what == "exp":
                        act.wait_ge(head_sig, hd + 1)
                        sc.activation(aa[:, m], rr[:, m], ACT.Exp, scale=sp8n[:, hd:hd + 1]).then_inc(a_done, 1)
                    else:
                        act.wait_ge(a_done, hd + 1)
                        sc.activation(rr[:, m], rr[:, m], ACT.Tanh, scale=sp4[:, hd:hd + 1]).then_inc(tanh_done, 1)
                if what == "root":
                    act.wait_ge(tanh_done, MC * (jc + 1))
                    sc.activation(bb[:], rr[:], ACT.Sqrt).then_inc(sqrt_done, 1)

            GATES = {}
            for jc in range(JC):
                q = Z.index(("lru", jc)) + 3
                GATES[q, 2] = ((jc, "sigmoid", (0, 1)),)
                GATES[q, 5] = ((jc, "sigmoid", (2, 3)),)
                GATES[q, 6] = ((jc, "exp", (0, 1)),)
                GATES[q, 7] = ((jc, "exp", (2, 3)), (jc, "tanh", (0, 1)))
                GATES[q + 1, 1] = ((jc, "tanh", (2, 3)),)
                GATES[q + 1, 2 if jc else 5] = ((jc, "root", ()),)

            def mixer_steps(q, j):
                if q == 1 and j < 4:
                    block_squares(1, j)
                if (q, j) in Z_TAKE:
                    z_take(Z_TAKE[q, j])
                if (q, j) in Z_SCALE:
                    z_scale(Z_SCALE[q, j])
                for jc, what, ms in GATES.get((q, j), ()):
                    gates(jc, what, ms)
                if (q, j) in Y_PART:
                    n = Y_PART[q, j]
                    act.wait_ge(y_ready, n + 1)
                    sc.copy(hT_hi[:, MC * n:MC * n + MC, :], yy[:]).then_inc(y_hi, 1)

            ffn(0)
            hand_over(1)
            for q in range(1, NZ):
                for j in range(GP):
                    mixer_steps(q, j)
                    split(Place(starts["in"] + GP * q), j)
            for j in range(GP):
                mixer_steps(NZ, j)
                split(Place(starts["out"]), j)
            summed_chunks(starts["out"], GP, 3)
            ffn(1)
            last_square(2, 0)
            last_square(2, 1)

        @block.vector
        def _(dve):
            ve = nc.vector
            steps = [0]

            def chain(ins):
                steps[0] += 1
                ins.then_inc(step, 1)
                dve.wait_ge(step, steps[0])

            def split(pl, j):
                s = pl.slot(j)
                dve.wait_ge(hi_ready, pl.count(j))
                ve.tensor_tensor(w_lo[:, s], raw[:, s], w_hi[:, s].bitcast(f32), ALU.subtract
                                 ).then_inc(lo_ready, 1)

            def gain_bank(d, n, t):
                dve.wait_ge(sq_done, n * TOK + (TOK * NC * d + t + 1))
                dve.wait_ge(gpost_in, 16 * (d + 1))
                ve.tensor_tensor(bank(n * 2 + t), bank(n * 2 + t), gpost[:, columns(n)], ALU.mult
                                 ).then_inc(fg_done, 1)

            def post_norm(d, t):
                k = 1 if d == 1 else 4
                dve.wait_ge(sq_done, TOK * NC * d + TOK * (NC - 1) + t + 1)
                ve.reduce_sum(tot[:, 0, t:t + 1], sums[:, 0, t], axis=AX.X).then_inc(tot_post, 1)
                dve.wait_ge(tot_post, TOK * d + t + 1)
                ve.tensor_scalar(mean[:, 0, t:t + 1], tot[:, 0, t:t + 1], k / D, k * EPS, ALU.mult, ALU.add
                                 ).then_inc(mean_post, 1)

            def update(d, n, t, c):
                dve.wait_ge(rstd_post, TOK * d + t + 1)
                dve.wait_ge(fg_done, TOK * NC * d + TOK * c + t + 1)
                ve.scalar_tensor_tensor(out=resid[:, t, columns(c)], in0=bank(2 * c + t),
                                        scalar=rstd[:, 0, t:t + 1], in1=resid[:, t, columns(c)],
                                        op0=ALU.mult, op1=ALU.add).then_inc(resid_new, 1)

            def block_lo(r, k):
                t, c = BLOCKS[k]
                dve.wait_ge(blk_hi, NBLK * r + k + 1)
                for m in range(MC):
                    f = MC * c + m
                    ins = ve.scalar_tensor_tensor(out=xT_lo[:, f, part(t)], in0=bank(2 * c + t, P, m * P),
                                                  scalar=cst[:, r * KD + f:r * KD + f + 1],
                                                  in1=xT_hi[:, f, part(t)].bitcast(f32),
                                                  op0=ALU.mult, op1=ALU.subtract)
                ins.then_inc(blk_lo, 1)

            def hand_over(r):
                pl = Place(starts[PHASE[r]])
                for what, n in order(LO_FIRST if r == 0 else LO):
                    if what == "split":
                        if n - 1 in POOL_SPLITS[r]:
                            dve.wait_ge(lo_ready, pl.count(n - 1))
                        split(pl, n)
                    elif what == "lo":
                        block_lo(r, n)
                    elif what == "post":
                        post_norm(r - 1, n)
                    elif what == "bank":
                        gain_bank(r - 1, NC - 1, n)
                    else:
                        update(r - 1, n, *BLOCKS[n])

            def pre_norm(r):
                dve.wait_ge(blk_sq, NBLK * (r + 1))
                ve.reduce_sum(tot[:, 1, :], sums[:, 1], axis=AX.X).then_inc(tot_pre, 1)
                dve.wait_ge(tot_pre, r + 1)
                ve.tensor_scalar(mean[:, 1, :], tot[:, 1, :], 1 / D, EPS, ALU.mult, ALU.add).then_inc(mean_pre, 1)

            def hidden(f, c, summed):
                dve.wait_ge(w_used, summed)
                dve.wait_ge(silu_done, c * TOK + (f * FC * TOK + TOK))
                for t in range(TOK):
                    ve.scalar_tensor_tensor(out=hid[:, t], in0=bank(2 + t), scalar=rstd[:, 1, t:t + 1],
                                            in1=act_g[:, t], op0=ALU.mult, op1=ALU.mult).then_inc(hid_done, 1)

            def hidden_lo(f, c):
                tiles = slice(c * MC, c * MC + MC) if isinstance(c, int) else ds(c * MC, MC)
                for t in range(TOK):
                    dve.wait_ge(hT_hi_done, c * TOK + (f * FC * TOK + t + 1))
                    ve.tensor_tensor(hT_lo[:, tiles, part(t)], bank(XP + t).rearrange("p (m q) -> p m q", q=P),
                                     hT_hi[:, tiles, part(t)].bitcast(f32), ALU.subtract).then_inc(hT_lo_done, 1)

            def up_groups(f, pl, c, js, tail):
                for j in js:
                    if tail and j == 3:
                        hidden(f, c - 1, pl.count(-1))
                    if tail and j == GP:
                        hidden_lo(f, c - 1)
                    if not tail and j == GP + 4:
                        pre_norm(2 * f)
                    if not tail and f == 0 and j in (GP + 5, GP + 7):
                        softplus(("lambda", "series")[j == GP + 7])
                    split(pl, j)

            def summed_chunks(d, g0, n_groups, hook):
                with dve.Fori(0, NC - 1) as it:
                    for j in range(n_groups):
                        if j == hook:
                            for t in range(TOK):
                                gain_bank(d, it, t)
                        split(Place(g0 + n_groups, it, n_groups), j)

            def ffn(f):
                up, down = starts[f"up{f + 1}"], starts[f"down{f + 1}"]
                hand_over(2 * f)
                up_groups(f, Place(up), 0, range(GP, 2 * GP), False)
                if f == 0:
                    softplus("end")
                with dve.Fori(0, FC - 1) as it:
                    up_groups(f, Place(up + 2 * GP, it, 2 * GP), it + 1, range(2 * GP), True)
                for j in range(GF):
                    if j == 3:
                        hidden(f, FC - 1, down)
                    if j == GP:
                        hidden_lo(f, FC - 1)
                    split(Place(down), j)
                summed_chunks(2 * f, down, GF, GP + 2)

            def softplus(what):
                s, q, neg, w, w2 = (soft[:, n] for n in range(5))
                if what == "lambda":
                    dve.wait_ge(small_xp, 2)
                    ve.tensor_copy(cst[:, KD:], bank(7, NB)).then_inc(cst_ready, 1)
                    dve.wait_ge(cst_ready, 2)
                    lam_t = cst[:, LAM:LAM + HEADS]
                    chain(ve.tensor_scalar(neg, lam_t, -1.0, None, ALU.mult))
                    ve.tensor_tensor(s, lam_t, neg, ALU.min).then_inc(lam_neg, 1)
                elif what == "series":
                    dve.wait_ge(lam_sig, 1)
                    chain(ve.tensor_scalar(w, q, -1.0, 2.0, ALU.mult, ALU.add))
                    chain(ve.reciprocal(w, w))
                    chain(ve.tensor_tensor(w, w, q, ALU.mult))
                    chain(ve.tensor_tensor(w2, w, w, ALU.mult))
                    chain(ve.tensor_scalar(s, w2, 1 / 17, None, ALU.mult))
                    for k in range(7, 0, -1):
                        chain(ve.scalar_tensor_tensor(out=s, in0=s, scalar=1 / (2 * k + 1), in1=w2,
                                                      op0=ALU.add, op1=ALU.mult))
                else:
                    chain(ve.scalar_tensor_tensor(out=s, in0=s, scalar=1.0, in1=w, op0=ALU.add, op1=ALU.mult))
                    chain(ve.tensor_scalar(neg, neg, 0.0, 4.0, ALU.max, ALU.mult))
                    chain(ve.scalar_tensor_tensor(out=sp4[:], in0=s, scalar=8.0, in1=neg,
                                                  op0=ALU.mult, op1=ALU.add))
                    chain(ve.tensor_scalar(sp8n[:], sp4[:], -2.0, None, ALU.mult))

            def conv(dst, m, first_col, taps, weights, bias, done=None):
                for k in range(taps):
                    src = xpad[:, m, first_col + k:first_col + k + T]
                    wk = cst[:, weights + HEADS * k:weights + HEADS * k + 1]
                    if k == 0 and bias is not None:
                        ins = ve.tensor_scalar(dst[:, m], src, wk, bias, ALU.mult, ALU.add)
                    elif k == 0:
                        ins = ve.tensor_scalar(dst[:, m], src, wk, None, ALU.mult)
                    else:
                        ins = ve.scalar_tensor_tensor(out=dst[:, m], in0=src, scalar=wk, in1=dst[:, m],
                                                      op0=ALU.mult, op1=ALU.add)
                    if k == taps - 1 and done is not None:
                        ins.then_inc(done, 1)
                    else:
                        chain(ins)

            def lru_conv(jc, m):
                hd = jc * MC + m
                dve.wait_ge(z_taken, 2 * Z.index(("lru", jc)) + 2)
                if jc:
                    dve.wait_ge(head_mm, MC * jc)
                dve.wait_ge(pads_set, 1)
                conv(xc, m, 0, TAPS_A, CONV_W + hd, cst[:, CONV_B + hd:CONV_B + hd + 1], xc_ready)

            def lru(jc, what):
                if what == "ix":
                    dve.wait_ge(head_sig, jc * MC + MC)
                    chain(ve.tensor_tensor(ii[:], ii[:], xc[:], ALU.mult))
                elif what == "b":
                    dve.wait_ge(sqrt_done, jc + 1)
                    chain(ve.scalar_tensor_tensor(out=bb[:], in0=aa[:], scalar=1.0, in1=bb[:],
                                                  op0=ALU.add, op1=ALU.mult))
                    chain(ve.tensor_tensor(bb[:], bb[:], ii[:], ALU.mult))
                elif what[0] == "s":
                    for m in (int(what[1]), int(what[1]) + 1):
                        chain(ve.tensor_tensor_scan(out=yc[:, m], data0=aa[:, m], data1=bb[:, m], initial=0.0,
                                                    op0=ALU.mult, op1=ALU.add))
                else:
                    if jc:
                        dve.wait_ge(y_lo, jc)
                    ve.tensor_tensor(yy[:], yc[:], gl[jc][:], ALU.mult).then_inc(y_ready, 1)

            def z_take(q):
                kind, jc = Z[q]
                if kind not in ("x", "b"):
                    return
                dve.wait_ge(z_xp, q + 1)
                if kind == "x":
                    dve.wait_ge(z_taken, 2 * q)
                elif kind == "b":
                    dve.wait_ge(y_lo, 2 + jc)
                for h in range(2):
                    src = bank(XP + h).rearrange("p (m q) -> p m q", q=T)
                    dst = slice(2 * h, 2 * h + 2)
                    if kind == "x":
                        ve.tensor_tensor(xpad[:, dst, pad:], src, cc[:, dst], ALU.mult).then_inc(z_taken, 1)
                    else:
                        ve.tensor_tensor(yy[:, dst], src, yc[:, dst], ALU.mult).then_inc(z_taken, 1)
                if kind == "b":
                    dve.wait_ge(z_taken, 2 * q + 2)
                    dve.sem_inc(y_ready, 1)

            def short_conv(jc, m):
                ft = jc * MC + m
                dve.wait_ge(z_taken, 2 * Z.index(("x", jc)) + 2)
                dve.wait_ge(y_ready, 2 + jc)
                conv(yc, m, pad + 1 - TAPS_B, TAPS_B, SC_W + ft, None)

            LRU_CONV = {(Z.index(("lru", jc)) + 2, 1 + m): (jc, m) for jc in range(JC) for m in range(MC)}
            LRU = {(5, 0): (0, "ix"), (5, 7): (0, "b"), (6, 0): (0, "s0"), (6, 1): (0, "s2"), (6, 2): (0, "y"),
                   (7, 0): (1, "ix"), (7, 3): (1, "b"), (7, 4): (1, "s0"), (7, 5): (1, "s2"), (7, 6): (1, "y")}
            SHORT = {(7, 7): ((0, 0),), (8, 0): ((0, 1),), (8, 1): ((0, 2),), (8, 2): ((0, 3),),
                     (NZ, 0): ((1, 0),), (NZ, 1): ((1, 1),), (NZ, 2): ((1, 2),), (NZ, 3): ((1, 3),)}

            def mixer_steps(q, j):
                if (q, j) == (1, 4):
                    pre_norm(1)
                if (q, j) in Z_TAKE:
                    z_take(Z_TAKE[q, j])
                if (q, j) in LRU:
                    lru(*LRU[q, j])
                if (q, j) in LRU_CONV:
                    lru_conv(*LRU_CONV[q, j])
                for jc, m in SHORT.get((q, j), ()):
                    short_conv(jc, m)
                if (q, j) in Y_PART:
                    n = Y_PART[q, j]
                    dve.wait_ge(y_hi, n + 1)
                    ve.tensor_tensor(hT_lo[:, MC * n:MC * n + MC, :], yy[:],
                                     hT_hi[:, MC * n:MC * n + MC, :].bitcast(f32), ALU.subtract).then_inc(y_lo, 1)

            dve.wait_ge(small_xp, 1)
            ve.tensor_copy(cst[:, 0:KD], bank(6, KD)).then_inc(cst_ready, 1)
            dve.wait_ge(cst_ready, 1)

            ffn(0)
            hand_over(1)
            for q in range(1, NZ):
                for j in range(GP):
                    mixer_steps(q, j)
                    split(Place(starts["in"] + GP * q), j)
            for j in range(GP):
                mixer_steps(NZ, j)
                split(Place(starts["out"]), j)
            summed_chunks(1, starts["out"], GP, 5)
            ffn(1)
            for t in range(TOK):
                post_norm(2, t)
                gain_bank(2, NC - 1, t)
                for c in range(NC):
                    update(2, NC * t + c, t, c)

        @block.tensor
        def _(pe):
            te = nc.tensor

            def products(pl, j, hi, lo, kt, t, dst, start, stop):
                s = pl.slot(j)
                for k in range(GK):
                    xh, xl = hi[:, kt + k, part(t)], lo[:, kt + k, part(t)]
                    te.matmul(dst, xh, w_hi[:, s, k], start=start and k == 0, stop=False)
                    te.matmul(dst, xh, w_lo[:, s, k], start=False, stop=False)
                    last = te.matmul(dst, xl, w_hi[:, s, k], start=False, stop=stop and k == GK - 1)
                return last

            def group(pl, j, hi, lo, jk, n_groups, banks):
                pe.wait_ge(lo_ready, pl.count(j))
                for t in range(TOK):
                    last = products(pl, j, hi, lo, GK * jk, t, banks[t], jk == 0, jk == n_groups - 1)
                last.then_inc(w_used, 1)

            def last_groups(pl, j0, hi, lo, n_groups, banks, at_group=None, r=None):
                for t in range(TOK):
                    for j in range(j0, n_groups):
                        if r and t == 1 and j == j0 + 2:
                            block_transpose(r, 0)
                        if t == 0:
                            if at_group:
                                at_group(j)
                            pe.wait_ge(lo_ready, pl.count(j))
                        last = products(pl, j, hi, lo, GK * j, t, banks[t], j == 0, j == n_groups - 1)
                        if t == TOK - 1:
                            last.then_inc(w_used, 1)
                    if t == 0:
                        last.then_inc(tok0_done, 1)

            def block_transpose(r, k):
                t, c = BLOCKS[k]
                if r:
                    pe.wait_ge(resid_new, NBLK * (r - 1) + k + 1)
                else:
                    pe.wait_ge(x_in[k], 16)
                for m in range(MC):
                    last = te.transpose(bank(2 * c + t, P, m * P), resid[:, t, c * W + m * P:c * W + m * P + P],
                                        ident[:])
                last.then_inc(blk_xp, 1)

            def first_chunk(r):
                pl = Place(starts[PHASE[r]])

                def mm(k, h):
                    t, c = BLOCKS[k]
                    j = 2 * c + h
                    pe.wait_ge(lo_ready, pl.count(j))
                    pe.wait_ge(blk_lo, NBLK * r + k + 1)
                    last = products(pl, j, xT_hi, xT_lo, GK * j, t, bank(t), j == 0, j == GP - 1)
                    if t == TOK - 1:
                        last.then_inc(w_used, 1)

                if not r:
                    block_transpose(r, 0)
                block_transpose(r, 1)
                mm(0, 0)
                mm(0, 1)
                block_transpose(r, 2)
                mm(1, 0)
                block_transpose(r, 3)
                mm(1, 1)
                for k in range(2, NBLK):
                    mm(k, 0)
                    if k + 2 < NBLK:
                        block_transpose(r, k + 2)
                    mm(k, 1)

            def summed_chunks(g0, n_groups, r):
                def chunk(pl, n, r=None):
                    banks = (bank(n * 2), bank(n * 2 + 1))
                    for j in range(n_groups - 4):
                        group(pl, j, hT_hi, hT_lo, j, n_groups, banks)
                    last_groups(pl, n_groups - 4, hT_hi, hT_lo, n_groups, banks, r=r)

                with pe.Fori(0, NC - 2) as it:
                    chunk(Place(g0 + n_groups, it, n_groups), it + 1)
                chunk(Place(g0 + (NC - 1) * n_groups), NC - 1, r)

            def hidden_transpose(f, c):
                for t in range(TOK):
                    pe.wait_ge(hid_done, c * TOK + (f * FC * TOK + t + 1))
                    for m in range(MC):
                        last = te.transpose(bank(XP + t, P, m * P), hid[:, t, m * P:m * P + P], ident[:])
                    last.then_inc(hid_xp, 1)

            def ffn(f):
                up, down = starts[f"up{f + 1}"], starts[f"down{f + 1}"]
                done = f * FC * TOK
                first_chunk(2 * f)
                if f == 0:
                    pe.wait_ge(small_b_in, 16 * 8)
                    te.transpose(bank(7, NB), small_b[:], ident[0:NB, 0:NB]).then_inc(small_xp, 1)
                for j in range(GP):
                    group(Place(up + GP), j, xT_hi, xT_lo, j, GP, (bank(2), bank(3)))
                with pe.Fori(0, FC - 1) as it:
                    pl = Place(up + 2 * GP, it, 2 * GP)
                    pe.wait_ge(silu_done, it * TOK + (done + TOK))
                    for j in range(GP):
                        group(pl, j, xT_hi, xT_lo, j, GP, (bank(0), bank(1)))
                        if j == 3:
                            hidden_transpose(f, it)
                    pe.wait_ge(hid_done, it * TOK + (done + TOK))
                    for j in range(GP):
                        group(pl, GP + j, xT_hi, xT_lo, j, GP, (bank(2), bank(3)))
                pe.wait_ge(silu_done, done + FC * TOK)
                pe.wait_ge(hT_lo_done, done + (FC - 1) * TOK)
                pl = Place(down)
                for j in range(GF - 4):
                    group(pl, j, hT_hi, hT_lo, j, GF, (bank(0), bank(1)))
                    if j == 3:
                        hidden_transpose(f, FC - 1)
                pe.wait_ge(hT_lo_done, done + FC * TOK)
                last_groups(pl, GF - 4, hT_hi, hT_lo, GF, (bank(0), bank(1)))
                pe.wait_ge(hid_done, done + FC * TOK)
                summed_chunks(down, GF, None if f else 1)

            def z_transpose(q):
                pe.wait_ge(z_out, TOK * (q + 1))
                if q:
                    pe.wait_ge(z_taken, 2 * q)
                for t in range(TOK):
                    for m in range(MC):
                        last = te.transpose(bank(XP + m // 2, P, (m % 2) * T + t * P),
                                            hid[:, t, m * P:m * P + P], ident[:])
                last.then_inc(z_xp, 1)

            def head_products(jc, ms):
                for m in ms:
                    hd = jc * MC + m
                    pe.wait_ge(xc_ready, hd + 1)
                    pe.wait_ge(heads_in, 32)
                    if hd >= 2:
                        pe.wait_ge(head_sig, hd - 1)
                    for n in range(2):
                        last = te.matmul(bank(HD + m % 2, T, n * T), w_ri[:, n, hd], xc[:, m],
                                         start=True, stop=True)
                    last.then_inc(head_mm, 1)

            HEADS_AT = {(Z.index(("lru", jc)) + dq, j): (jc, ms) for jc in range(JC)
                        for dq, j, ms in ((2, 6, (0, 1)), (3, 1, (2, 3)))}

            pe.wait_ge(pool_set, 3)
            pe.wait_ge(small_a_in, 16)
            te.transpose(bank(6, KD), small_a[:], ident[0:KD, 0:KD]).then_inc(small_xp, 1)
            pe.wait_ge(cst_ready, 1)

            ffn(0)
            first_chunk(1)
            for q in range(1, NZ):
                pl = Place(starts["in"] + GP * q)
                if q > 1:
                    pe.wait_ge(z_out, TOK * (q - 1))
                for j in range(GP):
                    group(pl, j, xT_hi, xT_lo, j, GP, (bank(2 * (q % 2)), bank(2 * (q % 2) + 1)))
                    if j == (4 if q == 1 else 3):
                        z_transpose(q - 1)
                    if (q, j) in HEADS_AT:
                        head_products(*HEADS_AT[q, j])
            pl = Place(starts["out"])
            pe.wait_ge(z_out, TOK * (NZ - 1))
            for j in range(4):
                if j % 2 == 0:
                    pe.wait_ge(y_lo, j // 2 + 1)
                group(pl, j, hT_hi, hT_lo, j, GP, (bank(0), bank(1)))
                if j == 1:
                    z_transpose(NZ - 1)

            def y_part(j):
                if j % 2 == 0:
                    pe.wait_ge(y_lo, j // 2 + 1)
            last_groups(pl, 4, hT_hi, hT_lo, GP, (bank(0), bank(1)), y_part)
            pe.wait_ge(head_sig, HEADS)
            summed_chunks(starts["out"], GP, 2)
            ffn(1)


_INS = ["x", "ffn1_pre_g", "ffn1_w_gate", "ffn1_w_up", "ffn1_w_down", "ffn1_post_g", "mix_pre_g", "w_in",
        "lru_conv_w", "lru_conv_b", "lru_w_r", "lru_b_r", "lru_w_i", "lru_b_i", "lru_lambda", "sc_conv_w",
        "w_out", "mix_post_g", "ffn2_pre_g", "ffn2_w_gate", "ffn2_w_up", "ffn2_w_down", "ffn2_post_g"]


def kernel(**inputs):
    import numpy as _np
    import concourse.bacc as _bacc
    from concourse import mybir as _mybir
    from concourse.bass_utils import run_bass_kernel_spmd as _run

    nc = _bacc.Bacc("TRN2", target_bir_lowering=False, num_devices=1)
    arrays, args = {}, []
    for name in _INS:
        a = _np.ascontiguousarray(inputs[name])
        arrays[f"in_{name}"] = a
        args.append(nc.dram_tensor(f"in_{name}", a.shape, _mybir.dt.from_np(a.dtype), kind="ExternalInput").ap())
    shape = tuple(inputs["x"].shape)
    args.append(nc.dram_tensor("out_0", shape, _mybir.dt.float32, kind="ExternalOutput").ap())
    hybrid_block_kernel(nc, *args)
    r = _run(nc, [arrays], core_ids=[0])
    return r.results[0]["out_0"]
```
